# Optimizing a Trainium2 kernel written in Bass

```python
import math
import jax, jax.numpy as jnp
from jax import lax
import numpy as np

D_MODEL = 1024
BATCH = 1
SEQ = 512
DEPTH = 2

HEAD_DIM = 64
MEM_LEN = 256
NORM_EPS = 1e-6
Q_BLOCK = 128
NEG_INF = -1e30
FORCE_SCORE = 1e9

NSA_HEADS = 8
NSA_KV_HEADS = 2
NSA_GROUP = NSA_HEADS // NSA_KV_HEADS
NSA_CMP_LEN = 32
NSA_CMP_STRIDE = 16
NSA_SEL_LEN = 64
NSA_TOP_N = 8
NSA_WINDOW = 512
NSA_Q_BLOCK = 64

SWA_HEADS = 8
SWA_KV_HEADS = 2
SWA_GROUP = SWA_HEADS // SWA_KV_HEADS
SWA_WINDOW = 128

MLA_HEADS = 8
MLA_Q_RANK = 256
MLA_KV_RANK = 128
MLA_NOPE_DIM = 64
MLA_ROPE_DIM = 32
MLA_V_DIM = 64
ROPE_THETA = 10000.0

FOX_HEADS = 8

XA_HEADS = 4

N_BRANCH = 4
BRANCH_WIDTH = 512
D_FF = ((8 * D_MODEL + 3 * 256 - 1) // (3 * 256)) * 256

NSA_Q_COLS = NSA_HEADS * HEAD_DIM
NSA_KV_COLS = NSA_KV_HEADS * HEAD_DIM
SWA_Q_COLS = SWA_HEADS * HEAD_DIM
SWA_KV_COLS = SWA_KV_HEADS * HEAD_DIM
FOX_COLS = FOX_HEADS * HEAD_DIM
IN_SPLITS = (NSA_Q_COLS, NSA_KV_COLS, NSA_KV_COLS, NSA_KV_COLS, NSA_KV_COLS, NSA_KV_COLS, NSA_KV_COLS, 3 * NSA_HEADS,
             SWA_Q_COLS, SWA_KV_COLS, SWA_KV_COLS,
             MLA_Q_RANK, MLA_KV_RANK, MLA_ROPE_DIM,
             FOX_COLS, FOX_COLS, FOX_COLS, FOX_HEADS)
IN_COLS = sum(IN_SPLITS)

kernel_name = "hybrid_nsa_swa_mla_fox_gated_trunk"

def rmsnorm(x, g):
    xf = x.astype(jnp.float32)
    y = xf * lax.rsqrt(jnp.mean(xf * xf, axis=-1, keepdims=True) + NORM_EPS)
    return (y * g.astype(jnp.float32)).astype(x.dtype)

def alibi_slopes(n):
    return jnp.asarray(2.0 ** (-8.0 * np.arange(1, n + 1) / n), dtype=jnp.float32)

def split_columns(z):
    offsets = np.cumsum(np.array(IN_SPLITS))[:-1].tolist()
    return jnp.split(z, offsets, axis=-1)

def rope(x, pos):
    half = x.shape[-1] // 2
    inv = ROPE_THETA ** (-jnp.arange(half, dtype=jnp.float32) / half)
    ang = pos[:, :, None, None] * inv
    cos, sin = jnp.cos(ang), jnp.sin(ang)
    xf = x.astype(jnp.float32)
    x1, x2 = xf[..., :half], xf[..., half:]
    return jnp.concatenate([x1 * cos - x2 * sin, x2 * cos + x1 * sin], axis=-1).astype(x.dtype)

def banded_attention(q, k, v, pos, window, slopes, sinks=None):
    B, S, Hk, G, Dh = q.shape
    nb = S // Q_BLOCK
    pad = window
    klen = pad + Q_BLOCK
    kp = jnp.pad(k, ((0, 0), (pad, 0), (0, 0), (0, 0)))
    vp = jnp.pad(v, ((0, 0), (pad, 0), (0, 0), (0, 0)))
    pp = jnp.pad(pos, ((0, 0), (pad, 0)))
    rel = np.arange(Q_BLOCK)[:, None] + pad - np.arange(klen)[None, :]
    band = jnp.asarray((rel >= 0) & (rel < window))
    scale = Dh ** -0.5

    def block(n):
        start = n * Q_BLOCK
        qn = lax.dynamic_slice_in_dim(q, start, Q_BLOCK, axis=1)
        pq = lax.dynamic_slice_in_dim(pos, start, Q_BLOCK, axis=1)
        kn = lax.dynamic_slice_in_dim(kp, start, klen, axis=1)
        vn = lax.dynamic_slice_in_dim(vp, start, klen, axis=1)
        pk = lax.dynamic_slice_in_dim(pp, start, klen, axis=1)
        valid = band & ((start + jnp.arange(klen)) >= pad)[None, :]
        s = jnp.einsum('bqhgd,bkhd->bhgqk', qn, kn).astype(jnp.float32) * scale
        s = s - slopes[None, :, :, None, None] * jnp.abs(pq[:, :, None] - pk[:, None, :])[:, None, None]
        s = jnp.where(valid, s, NEG_INF)
        if sinks is not None:
            sink = jnp.broadcast_to(sinks.astype(jnp.float32)[None, :, :, None, None], s.shape[:-1] + (1,))
            p = jax.nn.softmax(jnp.concatenate([s, sink], axis=-1), axis=-1)[..., :-1]
        else:
            p = jax.nn.softmax(s, axis=-1)
        return jnp.einsum('bhgqk,bkhd->bqhgd', p.astype(vn.dtype), vn)

    out = lax.map(block, jnp.arange(nb))
    return out.swapaxes(0, 1).reshape(B, S, Hk, G, Dh)

def causal_block_attention(q, k, v, scale, cum_logf=None):
    B, S, H, _ = q.shape
    nb = S // Q_BLOCK
    kpos = jnp.arange(S)

    def block(n):
        start = n * Q_BLOCK
        qn = lax.dynamic_slice_in_dim(q, start, Q_BLOCK, axis=1)
        s = jnp.einsum('bqhd,bkhd->bhqk', qn, k).astype(jnp.float32) * scale
        if cum_logf is not None:
            cq = lax.dynamic_slice_in_dim(cum_logf, start, Q_BLOCK, axis=1)
            s = s + cq.transpose(0, 2, 1)[:, :, :, None] - cum_logf.transpose(0, 2, 1)[:, :, None, :]
        tq = start + jnp.arange(Q_BLOCK)
        s = jnp.where(tq[:, None] >= kpos[None, :], s, NEG_INF)
        p = jax.nn.softmax(s, axis=-1)
        return jnp.einsum('bhqk,bkhd->bqhd', p.astype(v.dtype), v)

    out = lax.map(block, jnp.arange(nb))
    return out.swapaxes(0, 1).reshape(B, S, H, v.shape[-1])

def nsa_compress(x, cidx, w, pe):
    blocks = x[:, cidx] + pe[:, None, :].astype(x.dtype)
    return jnp.einsum('bclhd,lde->bche', blocks, w)

def nsa_mixer(q, k_c, v_c, k_s, v_s, k_w, v_w, gates, pos, cmp_w, cmp_pe):
    B, S, Hk, G, Dh = q.shape
    scale = Dh ** -0.5
    slopes = alibi_slopes(NSA_HEADS).reshape(Hk, G)
    n_c = (S - NSA_CMP_LEN) // NSA_CMP_STRIDE + 1
    cidx = np.arange(n_c)[:, None] * NSA_CMP_STRIDE + np.arange(NSA_CMP_LEN)[None, :]
    c_start, c_end = cidx[:, 0], cidx[:, -1]
    kc = nsa_compress(k_c, cidx, cmp_w[0], cmp_pe[0])
    vc = nsa_compress(v_c, cidx, cmp_w[1], cmp_pe[1])
    pc = pos[:, c_end]
    c_end_j = jnp.asarray(c_end)
    n_sel = S // NSA_SEL_LEN
    n_top = min(NSA_TOP_N, n_sel)
    sel_start = np.arange(n_sel) * NSA_SEL_LEN
    overlap = jnp.asarray(((c_start[:, None] < sel_start[None, :] + NSA_SEL_LEN) &
                           (c_end[:, None] >= sel_start[None, :])).astype(np.float32))
    ks_blk = k_s.reshape(B, n_sel, NSA_SEL_LEN, Hk, Dh).transpose(0, 3, 1, 2, 4)
    vs_blk = v_s.reshape(B, n_sel, NSA_SEL_LEN, Hk, Dh).transpose(0, 3, 1, 2, 4)
    ps_blk = pos.reshape(B, n_sel, NSA_SEL_LEN)
    b_ix = jnp.arange(B)[:, None, None, None]
    h_ix = jnp.arange(Hk)[None, None, :, None]
    jsel = jnp.arange(n_sel)
    Qb = NSA_Q_BLOCK

    def block(n):
        start = n * Qb
        qn = lax.dynamic_slice_in_dim(q, start, Qb, axis=1)
        pq = lax.dynamic_slice_in_dim(pos, start, Qb, axis=1)
        tq = start + jnp.arange(Qb)
        s = jnp.einsum('bqhgd,bchd->bqhgc', qn, kc).astype(jnp.float32) * scale
        s = s - slopes[None, None, :, :, None] * jnp.abs(pq[:, :, None] - pc[:, None, :])[:, :, None, None, :]
        cvis = (c_end_j[None, :] <= tq[:, None])[None, :, None, None, :]
        p = jax.nn.softmax(jnp.where(cvis, s, NEG_INF), axis=-1) * cvis
        o_c = jnp.einsum('bqhgc,bchd->bqhgd', p.astype(vc.dtype), vc)
        imp = jnp.einsum('bqhgc,cj->bqhj', p, overlap)
        jt = tq // NSA_SEL_LEN
        forced = (jsel[None, :] == 0) | (jsel[None, :] == jt[:, None]) | (jsel[None, :] == jt[:, None] - 1)
        causal = jsel[None, :] <= jt[:, None]
        imp = jnp.where(forced[None, :, None, :], FORCE_SCORE, imp)
        imp = jnp.where(causal[None, :, None, :], imp, NEG_INF)
        top_val, top_idx = lax.top_k(imp, n_top)
        ksel = ks_blk[b_ix, h_ix, top_idx]
        vsel = vs_blk[b_ix, h_ix, top_idx]
        psel = ps_blk[b_ix, top_idx]
        tok = top_idx[..., None] * NSA_SEL_LEN + jnp.arange(NSA_SEL_LEN)
        svis = (tok <= tq[None, :, None, None, None]) & (top_val > 0.5 * NEG_INF)[..., None]
        s2 = jnp.einsum('bqhgd,bqhnld->bqhgnl', qn, ksel).astype(jnp.float32) * scale
        s2 = s2 - slopes[None, None, :, :, None, None] * jnp.abs(pq[:, :, None, None, None] - psel)[:, :, :, None]
        s2 = jnp.where(svis[:, :, :, None], s2, NEG_INF)
        p2 = jax.nn.softmax(s2.reshape(B, Qb, Hk, G, n_top * NSA_SEL_LEN), axis=-1).reshape(s2.shape)
        o_s = jnp.einsum('bqhgnl,bqhnld->bqhgd', p2.astype(vsel.dtype), vsel)
        return o_c, o_s

    o_c, o_s = lax.map(block, jnp.arange(S // Qb))
    o_c = o_c.swapaxes(0, 1).reshape(B, S, Hk, G, Dh)
    o_s = o_s.swapaxes(0, 1).reshape(B, S, Hk, G, Dh)
    o_w = banded_attention(q, k_w, v_w, pos, NSA_WINDOW, slopes)
    return gates[..., 0:1] * o_c + gates[..., 1:2] * o_s + gates[..., 2:3] * o_w

def mla_mixer(c_q, c_kv, k_rope, pos, q_norm, w_q_up, kv_norm, w_kv_up):
    B, S, _ = c_q.shape
    q = (rmsnorm(c_q, q_norm) @ w_q_up).reshape(B, S, MLA_HEADS, MLA_NOPE_DIM + MLA_ROPE_DIM)
    kv = (rmsnorm(c_kv, kv_norm) @ w_kv_up).reshape(B, S, MLA_HEADS, MLA_NOPE_DIM + MLA_V_DIM)
    q_nope, q_rot = q[..., :MLA_NOPE_DIM], rope(q[..., MLA_NOPE_DIM:], pos)
    k_nope, v = kv[..., :MLA_NOPE_DIM], kv[..., MLA_NOPE_DIM:]
    k_rot = jnp.broadcast_to(rope(k_rope[:, :, None, :], pos), (B, S, MLA_HEADS, MLA_ROPE_DIM))
    qh = jnp.concatenate([q_nope, q_rot], axis=-1)
    kh = jnp.concatenate([k_nope, k_rot], axis=-1)
    return causal_block_attention(qh, kh, v, (MLA_NOPE_DIM + MLA_ROPE_DIM) ** -0.5)

def fox_mixer(q, k, v, f_logit, f_bias):
    log_f = jax.nn.log_sigmoid(f_logit.astype(jnp.float32) + f_bias.astype(jnp.float32))
    cum = jnp.cumsum(log_f, axis=1)
    return causal_block_attention(q, k, v, HEAD_DIM ** -0.5, cum)

def memory_cross_attention(h, mem_n, w_q, w_kv, w_o):
    B, S, _ = h.shape
    M = mem_n.shape[1]
    q = (h @ w_q).reshape(B, S, XA_HEADS, HEAD_DIM)
    kv = (mem_n @ w_kv).reshape(B, M, 2, XA_HEADS, HEAD_DIM)
    s = jnp.einsum('bshd,bmhd->bhsm', q, kv[:, :, 0]).astype(jnp.float32) * HEAD_DIM ** -0.5
    p = jax.nn.softmax(s, axis=-1)
    o = jnp.einsum('bhsm,bmhd->bshd', p.astype(kv.dtype), kv[:, :, 1])
    return o.reshape(B, S, XA_HEADS * HEAD_DIM) @ w_o

def setup_inputs(seed: int = 0) -> dict:
    key = jax.random.key(seed)
    ks = jax.random.split(key, 32)
    f32 = jnp.float32
    L, D = DEPTH, D_MODEL

    def nrm(k, shape, fan_in):
        return jax.random.normal(k, shape, f32) * fan_in ** -0.5

    def gain(k, shape):
        return 1.0 + 0.05 * jax.random.normal(k, shape, f32)

    offset = jax.random.randint(ks[2], (BATCH, 1), 0, 4096, dtype=jnp.int32)
    return {
        "x": jax.random.normal(ks[0], (BATCH, SEQ, D), f32),
        "mem": jax.random.normal(ks[1], (BATCH, MEM_LEN, D), f32),
        "positions": offset + jnp.arange(SEQ, dtype=jnp.int32)[None, :],
        "mix_norm_pre": gain(ks[3], (L, D)),
        "w_in": nrm(ks[4], (L, D, IN_COLS), D),
        "nsa_cmp_w": nrm(ks[5], (L, 2, NSA_CMP_LEN, HEAD_DIM, HEAD_DIM), NSA_CMP_LEN * HEAD_DIM),
        "nsa_cmp_pe": 0.1 * jax.random.normal(ks[6], (L, 2, NSA_CMP_LEN, HEAD_DIM), f32),
        "swa_sinks": 0.5 * jax.random.normal(ks[7], (L, SWA_HEADS), f32),
        "mla_q_norm": gain(ks[8], (L, MLA_Q_RANK)),
        "mla_w_q_up": nrm(ks[9], (L, MLA_Q_RANK, MLA_HEADS * (MLA_NOPE_DIM + MLA_ROPE_DIM)), MLA_Q_RANK),
        "mla_kv_norm": gain(ks[10], (L, MLA_KV_RANK)),
        "mla_w_kv_up": nrm(ks[11], (L, MLA_KV_RANK, MLA_HEADS * (MLA_NOPE_DIM + MLA_V_DIM)), MLA_KV_RANK),
        "fox_f_bias": 2.0 + 0.5 * jax.random.normal(ks[12], (L, FOX_HEADS), f32),
        "w_branch": nrm(ks[13], (L, N_BRANCH, BRANCH_WIDTH, D), BRANCH_WIDTH),
        "w_gate": nrm(ks[14], (L, N_BRANCH, D, D), D),
        "w_out": nrm(ks[15], (L, D, D), D),
        "mix_norm_post": gain(ks[16], (L, D)),
        "xa_norm_pre": gain(ks[17], (L, D)),
        "xa_mem_norm": gain(ks[18], (L, D)),
        "xa_w_q": nrm(ks[19], (L, D, XA_HEADS * HEAD_DIM), D),
        "xa_w_kv": nrm(ks[20], (L, D, 2 * XA_HEADS * HEAD_DIM), D),
        "xa_w_o": nrm(ks[21], (L, XA_HEADS * HEAD_DIM, D), XA_HEADS * HEAD_DIM),
        "xa_norm_post": gain(ks[22], (L, D)),
        "ffn_norm_pre": gain(ks[23], (L, D)),
        "ffn_w_in": nrm(ks[24], (L, D, 2 * D_FF), D),
        "ffn_w_out": nrm(ks[25], (L, D_FF, D), D_FF),
        "ffn_norm_post": gain(ks[26], (L, D)),
    }

def reference(x, mem, positions, mix_norm_pre, w_in, nsa_cmp_w, nsa_cmp_pe, swa_sinks,
              mla_q_norm, mla_w_q_up, mla_kv_norm, mla_w_kv_up, fox_f_bias, w_branch, w_gate,
              w_out, mix_norm_post, xa_norm_pre, xa_mem_norm, xa_w_q, xa_w_kv, xa_w_o,
              xa_norm_post, ffn_norm_pre, ffn_w_in, ffn_w_out, ffn_norm_post):
    B, S, D = x.shape
    pos = positions.astype(jnp.float32)
    swa_slopes = alibi_slopes(SWA_HEADS).reshape(SWA_KV_HEADS, SWA_GROUP)
    for l in range(DEPTH):
        h = rmsnorm(x, mix_norm_pre[l])
        (nq, nkc, nvc, nks, nvs, nkw, nvw, ng, sq, sk, sv,
         mcq, mckv, mkr, fq, fk, fv, ff) = split_columns(h @ w_in[l])
        kvh = lambda t: t.reshape(B, S, NSA_KV_HEADS, HEAD_DIM)
        y_nsa = nsa_mixer(nq.reshape(B, S, NSA_KV_HEADS, NSA_GROUP, HEAD_DIM),
                          kvh(nkc), kvh(nvc), kvh(nks), kvh(nvs), kvh(nkw), kvh(nvw),
                          jax.nn.sigmoid(ng).reshape(B, S, NSA_KV_HEADS, NSA_GROUP, 3),
                          pos, nsa_cmp_w[l], nsa_cmp_pe[l]).reshape(B, S, BRANCH_WIDTH)
        y_swa = banded_attention(sq.reshape(B, S, SWA_KV_HEADS, SWA_GROUP, HEAD_DIM),
                                 sk.reshape(B, S, SWA_KV_HEADS, HEAD_DIM),
                                 sv.reshape(B, S, SWA_KV_HEADS, HEAD_DIM),
                                 pos, SWA_WINDOW, swa_slopes,
                                 swa_sinks[l].reshape(SWA_KV_HEADS, SWA_GROUP)).reshape(B, S, BRANCH_WIDTH)
        y_mla = mla_mixer(mcq, mckv, mkr, pos, mla_q_norm[l], mla_w_q_up[l],
                          mla_kv_norm[l], mla_w_kv_up[l]).reshape(B, S, BRANCH_WIDTH)
        y_fox = fox_mixer(fq.reshape(B, S, FOX_HEADS, HEAD_DIM), fk.reshape(B, S, FOX_HEADS, HEAD_DIM),
                          fv.reshape(B, S, FOX_HEADS, HEAD_DIM), ff, fox_f_bias[l]).reshape(B, S, BRANCH_WIDTH)
        branches = (y_nsa, y_swa, y_mla, y_fox)
        merged = sum(jax.nn.sigmoid(h @ w_gate[l, i]) * (y @ w_branch[l, i]) for i, y in enumerate(branches))
        x = x + rmsnorm(merged @ w_out[l], mix_norm_post[l])
        hx = rmsnorm(x, xa_norm_pre[l])
        y = memory_cross_attention(hx, rmsnorm(mem, xa_mem_norm[l]), xa_w_q[l], xa_w_kv[l], xa_w_o[l])
        x = x + rmsnorm(y, xa_norm_post[l])
        hf = rmsnorm(x, ffn_norm_pre[l])
        gu = hf @ ffn_w_in[l]
        y = (jax.nn.silu(gu[..., :D_FF]) * gu[..., D_FF:]) @ ffn_w_out[l]
        x = x + rmsnorm(y, ffn_norm_post[l])
    return x


_drawn_inputs = setup_inputs


def setup_inputs(seed=0):
    import zlib

    import numpy as np

    out = dict(_drawn_inputs(seed))
    spreads = {}
    factors = {'swa_sinks': 10.077, 'mla_q_norm': 5.908, 'mla_kv_norm': 3.015}
    for name, (base, spread) in spreads.items():
        noise = np.random.default_rng([zlib.crc32(name.encode()), seed]).standard_normal(out[name].shape)
        drawn = base * np.exp(spread * noise) if base else spread * noise
        out[name] = __import__('jax').numpy.asarray(drawn.astype(out[name].dtype))
    for name, factor in factors.items():
        out[name] = (out[name] * factor).astype(out[name].dtype)
    return out
```

```python
import math
from contextlib import ExitStack

import concourse.bass as bass
import numpy as np
from concourse import mybir
from concourse.alu_op_type import AluOpType as ALU

F32 = mybir.dt.float32
F32R = mybir.dt.float32r
I32 = mybir.dt.int32
ACT = mybir.ActivationFunctionType

P = 128
S = 512
NT = S // P
D = 1024
KT = D // P
L = 2
M = 256
MT = M // P
EPS = 1e-6
HD = 64
H = 8
KVH = 2
XH = 4
CMP_LEN, CMP_STRIDE = 32, 16
NC = (S - CMP_LEN) // CMP_STRIDE + 1
NCP = NC + 1
WINDOW = 128
ROT = 32
QR, KVR = 256, 128
BW = 512
NB = 4
FF = ((8 * D + 3 * 256 - 1) // (3 * 256)) * 256
FK = FF // P
BIG = 1e30
NO_SINK = 3e38
CREDIT = 2

_cols = np.cumsum([0, 512, 128, 128, 128, 128, 128, 128, 24, 512, 128, 128, 256, 128, 32, 512, 512, 512, 8]).tolist()
(C_NQ, C_NKC, C_NVC, C_NKS, C_NVS, C_NKW, C_NVW, C_NG, C_SQ, C_SK, C_SV,
 C_MQ, C_MKV, C_MKR, C_FQ, C_FK, C_FV, C_FF, IN_COLS) = _cols
R_F, R_G, R_R = 0, 32, 64
R_END = R_R + ROT


def offsets(parts):
    at, out = 0, {}
    for name, n in parts:
        out[name] = at
        at += n
    return out, at


UNITS = [("misc", 1), ("nsa", 10), ("gate0", 8), ("br0", 4), ("swa", 6), ("gate1", 8), ("br1", 4), ("mla", 3),
         ("qup", 2), ("kvup", 2), ("gate2", 8), ("br2", 4), ("fox", 12), ("gate3", 8), ("br3", 4), ("wout", 8),
         ("xq", 2), ("xkv", 4), ("xo", 2), ("ffin", 2 * FK), ("ffout", 3 * KT)]
UB, NU = offsets(UNITS)
CHUNKS = [("misc", 1), ("nsa", 10), ("cmp", 2), ("gate0", 8), ("br0", 8), ("swa", 6), ("gate1", 8), ("br1", 8),
          ("mla", 3), ("qup", 8), ("kvup", 8), ("gate2", 8), ("br2", 8), ("fox", 12), ("gate3", 8), ("br3", 8),
          ("wout", 8), ("xq", 2), ("xkv", 4), ("xo", 8), ("ffin", 2 * FK), ("ffout", KT)]
CB, NCH = offsets(CHUNKS)
PASSES = [("cmp", 8), ("sel", 8), ("win", 8), ("swa", 8), ("mla", 8), ("fox", 8), ("xa", XH)]
HB, NHD = offsets(PASSES)
TURNS = [("v_cmp", 1), ("cmp", 32), ("v_sel", 1), ("sel", 32), ("v_win", 1), ("win", 32), ("y_nsa", 4),
         ("v_swa", 1), ("swa", 32), ("y_swa", 4), ("v_mla", 4), ("mla", 32), ("y_mla", 4),
         ("v_fox", 4), ("fox", 32), ("y_fox", 4), ("v_xa", 2), ("xa", 16), ("y_xa", 2)]
TB, NTN = offsets(TURNS)
NORMS = [("mix_pre", KT), ("mlaq", 2), ("mlakv", 1), ("mix_post", KT), ("xa_pre", KT), ("xa_post", KT),
         ("ffn_pre", KT), ("ffn_post", KT)]
SQB, NSQ = offsets(NORMS)
NB_OF = {name: i for i, (name, _) in enumerate(NORMS)}
NNORM = len(NORMS)
SPLITS = [("mix_pre", KT), ("mlaq", 2), ("mlakv", 1), ("merged", KT), ("xa_pre", KT), ("mem", KT), ("ffn_pre", KT),
          ("ffa", FK)]
SPB, NSP = offsets(SPLITS)
SPLIT_INS = [("mix_pre", KT), ("mlaq", 2), ("mlakv", 1), ("xa_pre", KT), ("mem", KT), ("ffn_pre", KT)]
SIB, NSI = offsets(SPLIT_INS)
NORM_STEPS = [("cmp", 24), ("sel", 32), ("win", 32), ("swa", 24), ("mla", 24), ("fox", 24), ("xa", 12)]
NSB, NMS = offsets(NORM_STEPS)
assert NU % 2 == 0 and NCH % 2 == 0 and NTN % 2 == 0 and NHD % 2 == 0, (NU, NCH, NTN, NHD)

GAINS = [("mix_pre", KT), ("mix_post", KT), ("xa_pre", KT), ("mem", KT), ("xa_post", KT), ("ffn_pre", KT),
         ("ffn_post", KT), ("mlaq", QR // P), ("mlakv", KVR // P)]
GB, NG = offsets(GAINS)
PARTS = [("cmp", 2), ("br0", 4), ("br1", 4), ("qup", 6), ("kvup", 6), ("br2", 4), ("br3", 4), ("xo", 6)]
PTB, NPT = offsets(PARTS)
NMG = (NB - 1) * KT
RESIDS = [("mix_post", KT), ("xa_post", KT), ("ffn_post", KT)]
RB, NRS = offsets(RESIDS)
PJ_Q = 0
PJ_K = {"cmp": 4, "sel": 6, "win": 8, "swa": 4, "fox": 4, "xa": 2}
PJ_V = {"cmp": 5, "sel": 7, "win": 9, "swa": 5, "fox": 8, "xa": 4}
PJ_CQ, PJ_KV, PJ_N = 8, 8, 16

TWO_PI = 2 * math.pi
MAGIC = 1.5 * 2.0 ** 23


def two_pi_parts():
    parts, rest = [], TWO_PI
    for _ in range(3):
        unit = 2.0 ** (math.floor(math.log2(rest)) - 6)
        parts.append(math.floor(rest / unit) * unit)
        rest -= parts[-1]
    return parts + [rest]


class Pass:

    def __init__(self, name, kdim=HD, grouped=False, slopes=False, sink=False, gate=None, filler=None, add=False,
                 heads=H):
        self.name, self.kdim, self.grouped, self.slopes, self.sink = name, kdim, grouped, slopes, sink
        self.gate, self.filler, self.add, self.heads = gate, filler, add, heads
        self.pairs = heads // 2
        self.outer = KVH if grouped else self.pairs
        self.inner = self.pairs // self.outer

    def keys(self, i):
        if self.name == "cmp":
            return 0, NCP
        if self.name == "xa":
            return 0, M
        lo = max(i - 1, 0) if self.name == "swa" else 0
        return lo * P, (i + 1 - lo) * P

    def tiles(self, i):
        k0, w = self.keys(i)
        return (1, w) if w < P else (w // P, P)


CMP = Pass("cmp", grouped=True, slopes=True, gate=0, filler=0)
SEL = Pass("sel", grouped=True, slopes=True, gate=1, add=True)
WIN = Pass("win", grouped=True, slopes=True, gate=2, add=True)
SWA = Pass("swa", grouped=True, slopes=True, sink=True, filler=1)
MLA = Pass("mla", kdim=HD + ROT, filler=2)
FOX = Pass("fox", kdim=HD + 1, filler=3)
XA = Pass("xa", heads=XH)


def build(nc, x, mem, positions, mix_norm_pre, w_in, nsa_cmp_w, nsa_cmp_pe, swa_sinks, mla_q_norm, mla_w_q_up,
          mla_kv_norm, mla_w_kv_up, fox_f_bias, w_branch, w_gate, w_out, mix_norm_post, xa_norm_pre, xa_mem_norm,
          xa_w_q, xa_w_kv, xa_w_o, xa_norm_post, ffn_norm_pre, ffn_w_in, ffn_w_out, ffn_norm_post, out):
    ctx = ExitStack()
    with ctx:
        def sb(name, shape, dt=F32, stack=ctx):
            return stack.enter_context(nc.sbuf_tensor(name, shape, dt))

        def sem(name):
            return ctx.enter_context(nc.semaphore(name))

        trunk = sb("trunk", [P, KT, S])
        w_f32 = sb("w_f32", [P, 2, 1024])
        w_hi = sb("w_hi", [P, 2, 1024], F32R)
        w_lo = sb("w_lo", [P, 2, 1024], F32R)
        h_hi = sb("h_hi", [P, KT, S], F32R)
        h_lo = sb("h_lo", [P, KT, S], F32R)
        wide = sb("wide", [P, KT, S])
        squares = sb("squares", [P, 2, S])
        work = sb("work", [P, 2, S])
        ident = sb("ident", [P, P])
        ones = sb("ones", [P, P])
        dist = sb("dist", [P, (NT * (NT + 1) // 2) * P])
        dist_swa = sb("dist_swa", [P, NT, 2 * P])
        dist_cmp = sb("dist_cmp", [P, NT, NCP])
        mask = sb("mask", [P, S])
        cos = sb("cos", [R_END, S])
        sin = sb("sin", [R_END, S])
        narrow = sb("narrow", [R_END, S])
        gains = sb("gains", [P, L * NG])
        cmp_pe = sb("cmp_pe", [P, L * 2 * CMP_LEN])
        f_bias = sb("f_bias", [H, L])
        head_plain = sb("head_plain", [P, H, 3])
        head_sink = sb("head_sink", [P, L * H, 3])
        head_now = sb("head_now", [P, 2, 3])
        q_scale = sb("q_scale", [P, H])
        consts = sb("consts", [P, 8])
        row_sees = sb("row_sees", [P, NT])
        gate_tanh = sb("gate_tanh", [P, NT, 3 * H])
        coef = sb("coef", [P, 4, NT, H])
        mean_sq = sb("mean_sq", [P, NT])
        rstd = sb("rstd", [P, NT])
        half_neg = sb("half_neg", [P, NT])
        neg_max = sb("neg_max", [P, 2, NT])
        row_sum = sb("row_sum", [P, 2, NT])
        sink_exp = sb("sink_exp", [P, 2, NT])
        norm4 = sb("norm4", [P, 2, 3, NT])
        ONE, NOSINK, ZERO4 = consts[:, 0:1], consts[:, 1:2], consts[:, 2:6]

        x_spill = nc.dram_tensor("x_spill", (P, KT, S), F32, kind="Internal").ap()
        mem_hat = nc.dram_tensor("mem_hat", (P, KT, M), F32, kind="Internal").ap()
        cum_spill = nc.dram_tensor("cum_spill", (2, H, S), F32, kind="Internal").ap()

        acc = [ctx.enter_context(nc.psum_tensor(f"acc{k}", [P, S], F32)) for k in range(2)]
        scores = [ctx.enter_context(nc.psum_tensor(f"scores{k}", [P, S], F32)) for k in range(2)]
        turn = [ctx.enter_context(nc.psum_tensor(f"turn{k}", [P, S], F32)) for k in range(2)]
        o_acc = [ctx.enter_context(nc.psum_tensor(f"o_acc{k}", [P, S], F32)) for k in range(2)]

        with ExitStack() as st:
            mem_in = sb("mem_in", [P, MT, D], stack=st)
            mem_t = sb("mem_t", [P, KT, M], stack=st)
            gain_rows = sb("gain_rows", [L * NG, P], stack=st)
            pe_rows = sb("pe_rows", [L * 2 * CMP_LEN, P], stack=st)
            pos_int = sb("pos_int", [P, S + NT], I32, stack=st)
            pos_row = sb("pos_row", [P, S + NT], stack=st)
            inv_row = sb("inv_row", [1, R_END], stack=st)
            ang = sb("ang", [R_END, 3, S], stack=st)
            mem_ms = sb("mem_ms", [P, 3, MT], stack=st)
        with ExitStack() as st:
            p_hi = sb("p_hi", [P, 2, S], F32R, st)
            p_lo = sb("p_lo", [P, 2, S], F32R, st)
            v_hi = sb("v_hi", [P, NT, BW], F32R, st)
            v_lo = sb("v_lo", [P, NT, BW], F32R, st)
            with ExitStack() as heads:
                q_hi = sb("q_hi", [P, 2, S], F32R, heads)
                q_lo = sb("q_lo", [P, 2, S], F32R, heads)
                k_hi = sb("k_hi", [P, 2, S], F32R, heads)
                k_lo = sb("k_lo", [P, 2, S], F32R, heads)
                q32 = sb("q32", [HD, S], F32, heads)
                k32 = sb("k32", [HD, S], F32, heads)
            with ExitStack() as after:
                y_hi = sb("y_hi", [P, BW // P, S], F32R, after)
                y_lo = sb("y_lo", [P, BW // P, S], F32R, after)
            sb("heads_place", [P, 10 * S], F32, st)
            with ExitStack() as mix:
                proj = sb("proj", [P, PJ_N, S], F32, mix)
                kg32 = sb("kg32", [HD, KVH, S], F32, mix)
                y_tok = sb("y_tok", [P, NT, BW], F32, mix)
            with ExitStack() as cross:
                proj_x = sb("proj_x", [P, 6, S], F32, cross)
                y_tok_x = sb("y_tok_x", [P, NT, XH * HD], F32, cross)
                m_hi = sb("m_hi", [P, KT, M], F32R, cross)
                m_lo = sb("m_lo", [P, KT, M], F32R, cross)
                m_f32 = sb("m_f32", [P, KT, M], F32, cross)
        with ExitStack() as st:
            a_hi = sb("a_hi", [P, FK, S], F32R, st)
            a_lo = sb("a_lo", [P, FK, S], F32R, st)

        wide_flat = wide[:, :, :].rearrange("p a b -> p (a b)")
        x_tok = wide_flat.rearrange("p (t d) -> p t d", t=NT)
        block_w = wide_flat.rearrange("p (l e) -> p l e", l=CMP_LEN)
        block_in = y_tok[:, :, :].rearrange("p a b -> p (a b)")[:, 0:CMP_LEN * NCP].rearrange(
            "p (l c) -> p l c", l=CMP_LEN)
        vc_feat = proj[:, 10, 0:NCP]
        logit, cum, cum_hi, cum_lo = (proj[0:H, 12 + n, :] for n in range(4))
        diag = squares[:, 0, :]
        SUMS, RBC = scores[0], scores[1]

        w_raw = [sem(f"w_raw{k}") for k in range(2)]
        misc_raw = sem("misc_raw")
        w_high = sem("w_high")
        w_ready = sem("w_ready")
        w_used = sem("w_used")
        part_ready = sem("part_ready")
        acc_free = [sem(f"acc_free{k}") for k in range(2)]
        staged = sem("staged")
        q_high = sem("q_high")
        qk_ready = sem("qk_ready")
        kg_ready = sem("kg_ready")
        scored = sem("scored")
        biased = sem("biased")
        exped = sem("exped")
        turned = sem("turned")
        turn_high = sem("turn_high")
        turn_ready = sem("turn_ready")
        applied = sem("applied")
        sink_ready = sem("sink_ready")
        normed = sem("normed")
        head_done = sem("head_done")
        squared = sem("squared")
        summed = sem("summed")
        ms_ready = sem("ms_ready")
        rstd_ready = sem("rstd_ready")
        diag_ready = sem("diag_ready")
        rbc_ready = sem("rbc_ready")
        split_in = sem("split_in")
        split_high = sem("split_high")
        split_ready = sem("split_ready")
        scaled_out = sem("scaled_out")
        trunk_new = sem("trunk_new")
        merged = sem("merged")
        ng_turned = sem("ng_turned")
        ng_tanh = sem("ng_tanh")
        ng_coef = sem("ng_coef")
        blocks_zero = sem("blocks_zero")
        blocks_in = sem("blocks_in")
        blocks_tok = sem("blocks_tok")
        rope = sem("rope")
        rot_high = sem("rot_high")
        rot_ready = sem("rot_ready")
        forget = sem("forget")
        forget_act = sem("forget_act")
        cum_out = sem("cum_out")
        cum_in = [sem(f"cum_in{k}") for k in range(2)]
        x_saved = sem("x_saved")
        x_back = sem("x_back")
        mem_back = sem("mem_back")
        ff_tanh = sem("ff_tanh")
        s_slot = sem("s_slot")
        s_const = sem("s_const")
        s_in = sem("s_in")
        s_rows = sem("s_rows")
        s_dve = sem("s_dve")
        s_pe = sem("s_pe")
        s_act = sem("s_act")
        s_angle = sem("s_angle")
        s_reduced = sem("s_reduced")
        s_far = sem("s_far")
        s_dist = sem("s_dist")
        s_masked = sem("s_masked")
        s_mem = sem("s_mem")
        s_mem_rstd = sem("s_mem_rstd")
        s_mem_turned = sem("s_mem_turned")
        s_mem_out = sem("s_mem_out")
        s_out = sem("s_out")

        def off(i):
            return i * (i + 1) // 2 * P

        def bias(ps, i):
            w = ps.keys(i)[1]
            if ps is CMP:
                return dist_cmp[:, i, :]
            if ps is SWA:
                return dist_swa[:, i, 0:w]
            if ps.slopes:
                return dist[:, off(i):off(i) + w]
            if ps is XA:
                return mask[:, 0:w]
            return mask[:, S - w:S]

        def raw_at(l, u, j):
            return l * (8 * NU) + j * 16 + 16 * (u // 2 + 1)

        def unit_at(l, u, j):
            return l * NU + 2 * j + u

        def free_at(l, c, q, j):
            return l * (NCH // 2) + q * j + (c // 2 + 1)

        def wait_apart(eng, signal, value):
            due = eng.to_reg(value)
            eng.wait_ge(s_const, 7)
            eng.wait_ge(signal, due)

        def wait_chunk_read(eng, l, name, c):
            c += CB[name]
            wait_apart(eng, acc_free[c % 2], free_at(l, c, 1, 0) + 1)

        def wait_chunk(eng, l, name, k, j, n):
            q = SHAPE[name.rstrip("0123")][0]
            if n == q - 1:
                eng.wait_ge(w_used, unit_at(l, UB[name] + k, j) + 3)
            else:
                eng.wait_ge(part_ready, l * NPT + (2 * (q - 1)) * j + (PTB[name] + k * (q - 1) + n + 1))

        def units(eng, name, body, first=0, count=None):
            n = (dict(UNITS)[name] if count is None else count)
            if n // 2 > 1:
                with eng.Fori(0, n // 2) as j:
                    body(first, j)
                    body(first + 1, j)
            elif n // 2 == 1:
                body(first, 0)
                body(first + 1, 0)
            if n % 2:
                body(first + n - 1, 0)

        def pairs(eng, ps, body):
            if ps.inner > 1:
                with eng.Fori(0, ps.outer) as g:
                    with eng.Fori(0, ps.inner) as n:
                        body(g * ps.inner + n, lambda e: g)
            else:
                with eng.Fori(0, ps.outer) as g:
                    body(g, lambda e: 2 * g + e)

        SHAPE = {"misc": (1, KT, R_END), "nsa": (1, KT, P), "swa": (1, KT, P), "mla": (1, KT, P), "fox": (1, KT, P),
                 "gate": (1, KT, P), "br": (2, BW // P, P), "qup": (4, QR // P, HD + ROT), "kvup": (4, KVR // P, P),
                 "wout": (1, KT, P), "xq": (1, KT, P), "xkv": (1, KT, P), "xo": (4, XH * HD // P, P),
                 "ffin": (1, KT, P)}
        FF_UNITS = [8, 8, FK - 16]

        block = ctx.enter_context(nc.Block())

        @block.sync
        def _(sp):
            sp.dma_start(x_tok, x[0].rearrange("(t p) d -> p t d", p=P)).then_inc(s_in, 16)
            sp.dma_start(mem_in[:, :, :], mem[0].rearrange("(t p) d -> p t d", p=P)).then_inc(s_in, 16)

            w_in_v = w_in.rearrange("l (k p) n -> l p k n", p=P)
            gate_v = w_gate.rearrange("l b (k p) n -> l b p k n", p=P)
            branch_v = w_branch.rearrange("l b (k p) n -> l b p k n", p=P)
            q_up_v = mla_w_q_up.rearrange("l (k p) n -> l p k n", p=P)
            kv_up_v = mla_w_kv_up.rearrange("l (k p) n -> l p k n", p=P)
            out_v = w_out.rearrange("l (k p) n -> l p k n", p=P)
            xq_v = xa_w_q.rearrange("l (k p) n -> l p k n", p=P)
            xkv_v = xa_w_kv.rearrange("l (k p) n -> l p k n", p=P)
            xo_v = xa_w_o.rearrange("l (k p) n -> l p k n", p=P)
            ff_in_v = ffn_w_in.rearrange("l (k p) n -> l p k n", p=P)
            ff_out_v = ffn_w_out.rearrange("l (k p) n -> l p k n", p=P)

            def slot(u, kts, cols):
                return w_f32[:, u % 2, 0:kts * cols].rearrange("p (k n) -> p k n", k=kts)

            def load(l, name, k, j, src, kts, cols):
                u = UB[name] + k
                sp.wait_ge(w_ready, unit_at(l, u, j) + 1)
                sp.dma_start(slot(u, kts, cols), src).then_inc(w_raw[u % 2], 16)

            sp.wait_ge(s_slot, 1)
            with sp.Fori(0, L) as l:
                u = UB["misc"]
                sp.wait_ge(w_ready, unit_at(l, u, 0) + 1)
                s3 = slot(u, KT, P)
                sp.dma_start(s3[:, :, R_R:R_END], w_in_v[l, :, :, C_MKR:C_FQ]).then_inc(w_raw[u % 2], 16)
                with nc.allow_non_contiguous_dma(reason="narrow projections"):
                    sp.dma_start(s3[:, :, R_F:R_F + H], w_in_v[l, :, :, C_FF:IN_COLS]).then_inc(misc_raw, 16)
                    sp.dma_start(s3[:, :, R_G:R_G + 3 * H], w_in_v[l, :, :, C_NG:C_SQ]).then_inc(misc_raw, 16)

                def w_cols(view, name, c0):
                    def body(k, j):
                        load(l, name, k, j, view[:, :, bass.ds(c0 + k * P + j * (2 * P), P)], KT, P)
                    units(sp, name, body)

                def gate(b):
                    w_cols(gate_v[l, b], f"gate{b}", 0)

                def branch(b):
                    def body(k, j):
                        load(l, f"br{b}", k, j, branch_v[l, b, :, :, bass.ds(k * 256 + j * 512, 256)], BW // P, 256)
                    units(sp, f"br{b}", body)

                w_cols(w_in_v[l], "nsa", C_NQ)
                gate(0)
                branch(0)
                w_cols(w_in_v[l], "swa", C_SQ)
                gate(1)
                branch(1)
                w_cols(w_in_v[l], "mla", C_MQ)
                w = 4 * (HD + ROT)
                units(sp, "qup", lambda k, j: load(l, "qup", k, j, q_up_v[l, :, :, k * w:(k + 1) * w], QR // P, w))
                units(sp, "kvup", lambda k, j: load(l, "kvup", k, j, kv_up_v[l, :, :, k * 512:(k + 1) * 512], 1, 512))
                gate(2)
                branch(2)
                w_cols(w_in_v[l], "fox", C_FQ)
                gate(3)
                branch(3)
                w_cols(out_v[l], "wout", 0)
                w_cols(xq_v[l], "xq", 0)
                w_cols(xkv_v[l], "xkv", 0)
                units(sp, "xo", lambda k, j: load(l, "xo", k, j, xo_v[l, :, :, k * 512:(k + 1) * 512], 2, 512))
                units(sp, "ffin", lambda k, j: load(l, "ffin", k, j, ff_in_v[l, :, :, bass.ds(k * FF + j * P, P)],
                                                    KT, P))
                with sp.Fori(0, KT // 2) as c:
                    for half in range(2):
                        k0 = 0
                        for n, kts in enumerate(FF_UNITS):
                            load(l, "ffout", 3 * half + n, 3 * c,
                                 ff_out_v[l, :, k0:k0 + kts, bass.ds(c * (2 * P) + half * P, P)], kts, P)
                            k0 += kts
            for t in range(NT):
                sp.wait_ge(s_act, KT + 2 * (t + 1))
                sp.dma_start(out[0].rearrange("(t p) d -> p t d", p=P)[:, t, :], x_tok[:, t, :]).then_inc(s_out, 16)
            sp.wait_ge(s_out, 16 * NT)

        @block.gpsimd
        def _(pool):
            pool.memset(w_f32[:, 0, :], 0.0).then_inc(s_slot, 1)
            with nc.allow_non_contiguous_dma(reason="small inputs"):
                for name, vec in (("mix_pre", mix_norm_pre), ("mix_post", mix_norm_post), ("xa_pre", xa_norm_pre),
                                  ("mem", xa_mem_norm), ("xa_post", xa_norm_post), ("ffn_pre", ffn_norm_pre),
                                  ("ffn_post", ffn_norm_post), ("mlaq", mla_q_norm), ("mlakv", mla_kv_norm)):
                    n = vec.shape[1] // P
                    for l in range(L):
                        r = l * NG + GB[name]
                        pool.dma_start(gain_rows[r:r + n, :], vec[l].rearrange("(k p) -> k p", p=P)).then_inc(s_rows, 16)
                for h in range(KVH):
                    pool.dma_start(pe_rows[:, h * HD:(h + 1) * HD],
                                   nsa_cmp_pe.rearrange("l c n d -> (l c n) d")).then_inc(s_rows, 16)
                pool.dma_start(pos_int[:, 0:S], positions[0:1, :].to_broadcast([P, S])).then_inc(s_rows, 16)
                pool.dma_start(pos_int[:, S:S + NT], positions[0].rearrange("(t p) -> p t", p=P)).then_inc(s_rows, 16)
                pool.dma_start(f_bias[:, :], fox_f_bias.rearrange("l h -> h l")).then_inc(s_rows, 16)
                pool.dma_start(head_sink[:, :, 2],
                               swa_sinks.rearrange("(o l) h -> o (l h)", o=1).to_broadcast([P, L * H])).then_inc(s_rows, 16)
            pool.memset(ident[:, :], 0.0).then_inc(s_const, 1)
            pool.memset(mask[:, :], 0.0).then_inc(s_const, 1)
            pool.memset(row_sees[:, :], 1.0).then_inc(s_const, 1)
            pool.memset(inv_row[:, 0:R_R], 0.0)
            for n in range(ROT // 2):
                f = float(np.float32(10000.0 ** (-n / (ROT // 2))))
                pool.memset(inv_row[:, R_R + n:R_R + n + 1], -f)
                pool.memset(inv_row[:, R_R + ROT // 2 + n:R_R + ROT // 2 + n + 1], f)
            pool.memset(ones[:, :], 1.0)
            pool.memset(half_neg[:, :], -0.5)
            pool.memset(consts[:, :], 0.0).then_inc(s_const, 1)
            pool.memset(coef[:, 3, :, :], 1.0)
            pool.memset(dist_cmp[:, :, NC:NCP], BIG)
            pool.memset(head_plain[:, :, 1:3], -NO_SINK)
            for h in range(H):
                slope = 2.0 ** -(h + 1)
                pool.memset(head_plain[:, h, 0:1], slope)
                pool.memset(q_scale[:, h:h + 1], -(HD ** -0.5) / slope)
                for l in range(L):
                    pool.memset(head_sink[:, l * H + h, 0:1], slope)
            pool.wait_ge(s_const, 4)
            pool.affine_select(out=ident[:, :], in_=ident[:, :], compare_op=ALU.not_equal, fill=1.0, base=0,
                               pattern=[[-1, P]], channel_multiplier=1).then_inc(s_const, 1)
            pool.memset(consts[:, 0:1], 1.0)
            pool.memset(consts[:, 1:2], NO_SINK)
            pool.affine_select(out=mask[:, :], in_=mask[:, :], compare_op=ALU.is_ge, fill=BIG, base=S - P,
                               pattern=[[-1, S]], channel_multiplier=1).then_inc(s_const, 1)
            pool.affine_select(out=row_sees[:, :], in_=row_sees[:, :], compare_op=ALU.is_ge, fill=0.0,
                               base=-(CMP_LEN - 1), pattern=[[P, NT]], channel_multiplier=1).then_inc(s_const, 1)
            pool.wait_ge(s_dist, 2 * NT)
            for i in range(NT):
                w = (i + 1) * P
                d = dist[:, off(i):off(i) + w]
                pool.affine_select(out=d, in_=d, compare_op=ALU.is_ge, fill=BIG, base=i * P, pattern=[[-1, w]],
                                   channel_multiplier=1).then_inc(s_masked, 1)
                c = dist_cmp[:, i, 0:NC]
                pool.affine_select(out=c, in_=c, compare_op=ALU.is_ge, fill=BIG, base=i * P - (CMP_LEN - 1),
                                   pattern=[[-CMP_STRIDE, NC]], channel_multiplier=1).then_inc(s_masked, 1)
            pool.wait_ge(s_masked, 2 * NT)
            for i in range(NT):
                k0, w = SWA.keys(i)
                pool.affine_select(out=dist_swa[:, i, 0:w], in_=dist[:, off(i) + k0:off(i) + k0 + w],
                                   compare_op=ALU.is_gt, fill=BIG, base=WINDOW - i * P + k0, pattern=[[1, w]],
                                   channel_multiplier=-1).then_inc(s_masked, 1)
            pool.wait_ge(s_mem, 3)
            pool.tensor_tensor(mem_ms[:, 2, :], mem_ms[:, 1, :], half_neg[:, 0:MT], ALU.pow).then_inc(s_mem_rstd, 1)
            pool.wait_ge(s_mem, 3 + MT + KT)
            pool.dma_start(mem_hat, mem_t[:, :, :]).then_inc(s_mem_out, 16)
            pool.wait_ge(s_mem_out, 16)

            def power(l, name):
                n = l * NNORM + NB_OF[name]
                wait_apart(pool, ms_ready, n + 1)
                pool.tensor_tensor(rstd[:, :], mean_sq[:, :], half_neg[:, :], ALU.pow).then_inc(rstd_ready, 1)

            with pool.Fori(0, L) as l:
                pool.wait_ge(s_act, KT)
                wait_apart(pool, trunk_new, l * NRS)
                pool.dma_start(x_spill, trunk[:, :, :]).then_inc(x_saved, 16)
                for kv in range(KVH):
                    a, b = kv * HD, (kv + 1) * HD
                    c, d = (1 - kv) * HD, (2 - kv) * HD
                    pool.memset(block_w[a:b, :, c:d], 0.0).then_inc(blocks_zero, 1)
                wait_apart(pool, blocks_zero, l * 2 + 2)
                power(l, "mix_pre")
                for cv in range(2):
                    if cv == 1:
                        wait_chunk_read(pool, l, "cmp", 0)
                    for kv in range(KVH):
                        a, b = kv * HD, (kv + 1) * HD
                        pool.dma_start(block_w[a:b, :, a:b],
                                       nsa_cmp_w[l, cv].rearrange("n d e -> d n e")).then_inc(blocks_in, 16)
                power(l, "mlaq")
                power(l, "mlakv")
                wait_apart(pool, forget, l * 8 + 8)
                pool.dma_start(cum_spill[0], cum_hi).then_inc(cum_out, 16)
                pool.dma_start(cum_spill[1], cum_lo).then_inc(cum_out, 16)
                with pool.Fori(0, FOX.pairs) as p:
                    for e in range(2):
                        pool.wait_ge(cum_out, l * 32 + 32)
                        pool.wait_ge(scored, (l * NHD + HB["fox"] + 2 * p + e) * 4 + 4)
                        for n, dst in enumerate((k_hi, k_lo)):
                            pool.dma_start(dst[HD:HD + 1, e, :].bitcast(F32),
                                           cum_spill[n, bass.ds(2 * p + e, 1), :]).then_inc(cum_in[e], 16)
                wait_apart(pool, split_ready, l * NSP + SPB["merged"] + KT)
                pool.dma_start(trunk[:, :, :], x_spill).then_inc(x_back, 16)
                wait_apart(pool, turn_ready, l * NTN + TB["y_fox"] + NT + 2)
                pool.dma_start(m_f32[:, :, :], mem_hat).then_inc(mem_back, 16)
                for name in ("mix_post", "xa_pre", "xa_post", "ffn_pre", "ffn_post"):
                    power(l, name)

        @block.scalar
        def _(act):
            def split_high_part(l, u, j):
                act.wait_ge(w_raw[u % 2], raw_at(l, u, j))
                act.wait_ge(w_used, unit_at(l, u, j) + 1)
                nc.scalar.activation(w_hi[:, u % 2, :], w_f32[:, u % 2, :], ACT.Copy).then_inc(w_high, 1)

            def next_unit(l, name, k, j):
                split_high_part(l, UB[name] + k + 1, j)

            def evac(l, name, k, j, n, out_ap, in_ap=None, func=ACT.Copy, scale=1.0):
                q = SHAPE[name.rstrip("0123")][0]
                c = CB[name] + k * q + n
                wait_chunk(act, l, name, k, j, n)
                src = acc[c % 2][0:out_ap.shape[0], 0:out_ap.shape[-1]]
                nc.scalar.activation(out_ap, src, func, scale=scale).then_inc(acc_free[c % 2], 1)

            def project(l, name, to, scale=1.0):
                q = SHAPE[name][0]

                def body(k, j):
                    next_unit(l, name, k, j)
                    for n in range(q):
                        evac(l, name, k, j, n, to(k * q + n, 2 * q * j), scale=scale)
                units(act, name, body)

            def square_chunk(l, name, c, src, scale=1.0):
                sq = l * NSQ + SQB[name] + c
                act.wait_ge(summed, sq + (2 if c == 0 else 1))
                if c == 0:
                    act.wait_ge(rbc_ready, l * NNORM + NB_OF[name])
                nc.scalar.activation(squares[:, c % 2, :], src, ACT.Square, scale=scale).then_inc(squared, 1)

            def split_chunk(l, name, c, dst, src):
                act.wait_ge(split_in, l * NSI + (SIB[name] + c + 1))
                nc.scalar.activation(dst, src, ACT.Copy).then_inc(split_high, 1)

            def norm_split(l, name, before):
                act.wait_ge(w_used, unit_at(l, UB[before], 0) + 2)
                for c in range(KT):
                    split_chunk(l, name, c, h_hi[:, c, :], work[:, c % 2, :])

            def turn_high_part(l, name, n, k, dst, src):
                t = l * NTN + n + (TB[name] + k)
                act.wait_ge(turned, t + 3)
                nc.scalar.activation(dst, src, ACT.Copy).then_inc(turn_high, 1)

            def value_turns(l, name, count, rows, tiles):
                for n in range(count):
                    bank = turn[(TB[name] + n) % 2]
                    turn_high_part(l, name, 0, n, v_hi[0:rows, 0:tiles, n * P:(n + 1) * P],
                                   bank[0:rows, 0:tiles * P].rearrange("p (t f) -> p t f", t=tiles))

            def out_turns(l, name, count):
                for f in range(count):
                    turn_high_part(l, name, 0, f, y_hi[:, f, :], turn[(TB[name] + f) % 2][:, :])

            def attend(l, ps):
                kd = ps.kdim

                def body(p, kv):
                    hd = l * NHD + HB[ps.name] + 2 * p
                    st = l * (4 * NHD) + 4 * HB[ps.name] + 8 * p
                    for e in range(2):
                        act.wait_ge(scored, 4 * hd + (4 * e + 4))
                        if ps is MLA:
                            src, s = proj[0:kd, bass.ds(2 * p + e, 1), :], 1.0
                        else:
                            buf = proj_x if ps is XA else proj
                            src = buf[e * HD:(e + 1) * HD, bass.ds(p, 1), :]
                            s = -(HD ** -0.5)
                        if ps.slopes:
                            s = q_scale[e * HD:(e + 1) * HD, bass.ds(2 * p + e, 1)]
                        rows = kd if ps is MLA else HD
                        nc.scalar.activation(q_hi[0:rows, e, :], src, ACT.Copy, scale=s).then_inc(q_high, 1)
                        if e == 0 and ps.filler is not None:
                            next_unit(l, f"gate{ps.filler}", 0, p)
                    for s in range(9):
                        if s < 8:
                            e, i = divmod(s, NT)
                            w = ps.keys(i)[1]
                            if i == 0:
                                act.wait_ge(head_done, hd + (e + 1))
                            act.wait_ge(biased, st + (s + 3))
                            nc.scalar.activation(work[:, s % 2, 0:w], work[:, s % 2, 0:w], ACT.Exp,
                                                 bias=neg_max[:, e, i:i + 1], scale=-1.0,
                                                 accum_out=row_sum[:, e, i:i + 1]).then_inc(exped, 1)
                            if ps.sink and i == NT - 1:
                                nc.scalar.activation(sink_exp[:, e, :], neg_max[:, e, :], ACT.Exp,
                                                     bias=head_now[:, e, 2:3]).then_inc(sink_ready, 1)
                        if s == 4 and ps.filler is not None:
                            evac(l, f"gate{ps.filler}", 0, p, 0, wide[:, bass.ds(2 * p, 1), :], func=ACT.Tanh, scale=0.5)
                            next_unit(l, f"gate{ps.filler}", 1, p)
                        if s > 0:
                            t = s - 1
                            n, rows = ps.tiles(t % NT)
                            act.wait_ge(applied, st + (t + 1))
                            turn_high_part(l, ps.name, 8 * p, t, p_hi[0:rows, t % 2, 0:n * P],
                                           turn[(TB[ps.name] + t) % 2][0:rows, 0:n * P])
                    if ps.filler is not None:
                        evac(l, f"gate{ps.filler}", 1, p, 0, wide[:, bass.ds(2 * p + 1, 1), :], func=ACT.Tanh, scale=0.5)
                pairs(act, ps, body)

            def branch(l, b):
                units(act, f"br{b}", lambda k, j: next_unit(l, f"br{b}", k, j))

            def out_chunk(l, name, k, j, n, scale, nm, c):
                ch = CB[name] + c
                wait_chunk(act, l, name, k, j, n)
                square_chunk(l, nm, c, acc[ch % 2][:, :], scale)
                nc.scalar.activation(wide[:, c, :], acc[ch % 2][:, :], ACT.Copy, scale=scale).then_inc(acc_free[ch % 2], 1)

            for c in range(KT):
                act.wait_ge(s_pe, c + 2)
                nc.scalar.activation(trunk[:, c, :], turn[(c + 1) % 2][:, :], ACT.Copy).then_inc(s_act, 1)
            act.wait_ge(s_reduced, 1)
            r = slice(R_R, R_END)
            nc.scalar.activation(sin[r, :], ang[r, 0, :], ACT.Sin)
            nc.scalar.activation(cos[r, :], ang[r, 1, :], ACT.Sin)

            with act.Fori(0, L) as l:
                act.wait_ge(misc_raw, l * 32 + 32)
                split_high_part(l, 0, 0)
                for c in range(KT):
                    act.wait_ge(trunk_new, l * NRS)
                    act.wait_ge(s_act, KT)
                    square_chunk(l, "mix_pre", c, trunk[:, c, :])
                norm_split(l, "mix_pre", "misc")
                next_unit(l, "misc", 0, 0)
                evac(l, "misc", 0, 0, 0, narrow[:, :])
                project(l, "nsa", lambda c, r_: proj[:, bass.ds(r_ + c, 1), :])
                act.wait_ge(ng_turned, l + 1)
                act.wait_ge(s_act, KT)
                nc.scalar.activation(gate_tanh[:, :, :], SUMS[:, 0:NT * 3 * H].rearrange("p (t g) -> p t g", t=NT),
                                     ACT.Tanh, scale=0.5).then_inc(ng_tanh, 1)
                value_turns(l, "v_cmp", 1, NCP, 1)
                attend(l, CMP)
                value_turns(l, "v_sel", 1, P, NT)
                attend(l, SEL)
                value_turns(l, "v_win", 1, P, NT)
                attend(l, WIN)
                out_turns(l, "y_nsa", BW // P)
                branch(l, 0)
                project(l, "swa", lambda c, r_: proj[:, bass.ds(r_ + c, 1), :])
                value_turns(l, "v_swa", 1, P, NT)
                attend(l, SWA)
                out_turns(l, "y_swa", BW // P)
                branch(l, 1)
                project(l, "mla", lambda c, r_: proj[:, bass.ds(r_ + (PJ_CQ + c), 1), :])
                wait_chunk_read(act, l, "mla", 1)
                wait_chunk_read(act, l, "mla", 2)
                for c in range(2):
                    square_chunk(l, "mlaq", c, proj[:, PJ_CQ + c, :])
                for c in range(2):
                    split_chunk(l, "mlaq", c, y_hi[:, c, :], work[:, c % 2, :])
                square_chunk(l, "mlakv", 0, proj[:, PJ_CQ + 2, :])
                split_chunk(l, "mlakv", 0, y_hi[:, 2, :], work[:, 0, :])
                project(l, "qup", lambda c, r_: proj[0:HD + ROT, c, :], scale=-(HD + ROT) ** -0.5)
                project(l, "kvup", lambda c, r_: proj[:, PJ_KV + c, :])
                act.wait_ge(rope, l * 36 + 36)
                for e in range(2):
                    nc.scalar.activation(k_hi[HD:HD + ROT, e, :], narrow[R_R:R_END, :], ACT.Copy).then_inc(rot_high, 1)
                value_turns(l, "v_mla", 4, P, NT)
                attend(l, MLA)
                out_turns(l, "y_mla", BW // P)
                branch(l, 2)
                project(l, "fox", lambda c, r_: proj[:, bass.ds(r_ + c, 1), :])
                act.wait_ge(forget, l * 8 + 2)
                nc.scalar.activation(cum_hi, logit, ACT.Exp, scale=-1.0).then_inc(forget_act, 1)
                act.wait_ge(forget_act, l * 2 + 1)
                nc.scalar.activation(cum_lo, cum_hi, ACT.Ln, bias=1.0).then_inc(forget_act, 1)
                value_turns(l, "v_fox", 4, P, NT)
                attend(l, FOX)
                out_turns(l, "y_fox", BW // P)
                branch(l, 3)
                act.wait_ge(w_used, unit_at(l, UB["wout"], 0) + 2)
                for c in range(KT):
                    act.wait_ge(merged, l * NMG + (NMG - KT + c + 1))
                    nc.scalar.activation(h_hi[:, c, :], trunk[:, c, :], ACT.Copy).then_inc(split_high, 1)
                for c in range(KT):
                    next_unit(l, "wout", c, 0)
                    out_chunk(l, "wout", c, 0, 0, 0.5, "mix_post", c)
                for c in range(KT):
                    act.wait_ge(trunk_new, l * NRS + (RB["mix_post"] + c + 1))
                    square_chunk(l, "xa_pre", c, trunk[:, c, :])
                norm_split(l, "xa_pre", "xq")
                for c in range(KT):
                    split_chunk(l, "mem", c, m_hi[:, c, :], work[:, c % 2, 0:M])
                project(l, "xq", lambda c, r_: proj_x[:, c, :])
                project(l, "xkv", lambda c, r_: proj_x[:, bass.ds(r_ + (2 + c), 1), 0:M])
                value_turns(l, "v_xa", 2, P, MT)
                attend(l, XA)
                out_turns(l, "y_xa", XH * HD // P)
                for c in range(KT):
                    if c % 4 == 0:
                        next_unit(l, "xo", c // 4, 0)
                    out_chunk(l, "xo", c // 4, 0, c % 4, 1.0, "xa_post", c)
                for c in range(KT):
                    act.wait_ge(trunk_new, l * NRS + (RB["xa_post"] + c + 1))
                    square_chunk(l, "ffn_pre", c, trunk[:, c, :])
                norm_split(l, "ffn_pre", "ffin")

                def ff(j, last=False):
                    next_unit(l, "ffin", 0, j)
                    c = CB["ffin"]
                    wait_chunk(act, l, "ffin", 0, j, 0)
                    act.wait_ge(split_ready, l * NSP + j + SPB["ffa"])
                    nc.scalar.activation(work[:, 0, :], acc[c % 2][:, :], ACT.Tanh, scale=0.5).then_inc(ff_tanh, 1)
                    next_unit(l, "ffin", 1, j)
                    act.wait_ge(acc_free[(c + 1) % 2], free_at(l, c + 1, 1, j) + 1)
                    nc.scalar.activation(a_hi[:, bass.ds(j, 1), :], work[:, 0, :], ACT.Copy).then_inc(split_high, 1)
                with act.Fori(0, FK) as j:
                    ff(j)
                for c in range(KT):
                    for n in range(3):
                        if c < KT - 1 or n < 2:
                            next_unit(l, "ffout", 3 * c + n, 0)
                    ch = CB["ffout"] + c
                    act.wait_ge(w_used, unit_at(l, UB["ffout"] + 3 * c + 2, 0) + 3)
                    square_chunk(l, "ffn_post", c, acc[ch % 2][:, :])
                    nc.scalar.activation(wide[:, c, :], acc[ch % 2][:, :], ACT.Copy).then_inc(acc_free[ch % 2], 1)

            for n in range(2 * NT):
                act.wait_ge(s_pe, KT + 1 + n + 1)
                nc.scalar.activation(x_tok[:, n // 2, (n % 2) * S:(n % 2 + 1) * S], turn[n % 2][:, :],
                                     ACT.Copy).then_inc(s_act, 1)

        @block.tensor
        def _(pe):
            pe.sem_inc(w_used, CREDIT)
            pe.sem_inc(scored, 2 * NT)
            pe.sem_inc(turned, CREDIT)
            pe.sem_inc(applied, CREDIT)
            pe.sem_inc(summed, CREDIT)

            def product(dst, lhs, rhs, n, count, last_sem=None):
                (lh, ll), (rh, rl) = lhs, rhs
                a, b = ((lh, rh), (lh, rl), (ll, rh))[n % 3]
                ins = nc.tensor.matmul(dst, a, b, start=(n == 0), stop=(n == count - 1))
                if last_sem is not None and n == count - 1:
                    ins.then_inc(last_sem, 1)
                return ins

            def weights(u, kts, cols, kt, c0, width):
                a = kt * cols + c0
                return w_hi[:, u % 2, a:a + width], w_lo[:, u % 2, a:a + width]

            def unit_terms(l, name, k, j, n0, n1, rhs, free=S):
                q, kts, width = SHAPE[name.rstrip("0123")]
                u = UB[name] + k
                per = 3 * kts
                for n in range(n0, n1):
                    m, r = divmod(n, per)
                    c = CB[name] + k * q + m
                    if n == 0:
                        pe.wait_ge(w_ready, unit_at(l, u, j) + 3)
                    if r == 0:
                        pe.wait_ge(acc_free[c % 2], free_at(l, c, q, j))
                    cols = P if name == "misc" else q * width
                    product(acc[c % 2][0:width, 0:free], weights(u, kts, cols, r // 3, m * width, width), rhs(r // 3),
                            r, per, w_used if m == q - 1 else part_ready)

            def whole_unit(l, name, k, j, rhs, free=S):
                q, kts, _ = SHAPE[name.rstrip("0123")]
                unit_terms(l, name, k, j, 0, 3 * q * kts, rhs, free)

            def h_rhs(kt):
                return h_hi[:, kt, :], h_lo[:, kt, :]

            def y_rhs(kt):
                return y_hi[:, kt, :], y_lo[:, kt, :]

            def sum_squares(l, name, c, n):
                sq = l * NSQ + SQB[name] + c
                pe.wait_ge(squared, sq + 1)
                for i in range(NT):
                    ins = nc.tensor.matmul(SUMS[:, i:i + 1], squares[:, c % 2, i * P:(i + 1) * P], ones[:, 0:1],
                                           start=(c == 0 and i == 0), stop=(c == n - 1), skip_group_check=True)
                ins.then_inc(summed, 1)

            def spread_rstd(l, name):
                pe.wait_ge(diag_ready, l * NNORM + NB_OF[name] + 1)
                nc.tensor.matmul(RBC[:, :], ones[:, :], diag, start=True, stop=True).then_inc(rbc_ready, 1)

            def norm(l, name):
                n = dict(NORMS)[name]
                for c in range(n):
                    sum_squares(l, name, c, n)
                spread_rstd(l, name)

            def turn_bank(l, name, n, k):
                t = TB[name] + k
                if name in ("v_cmp", "v_mla"):
                    wait_apart(pe, turn_ready, l * NTN + n + (t + 1))
                else:
                    pe.wait_ge(turn_ready, l * NTN + n + (t + 1))
                return turn[t % 2]

            def value_turns(l, name, count, src, rows=P, tiles=NT):
                for n in range(count):
                    bank = turn_bank(l, name, 0, n)
                    for t in range(tiles):
                        ins = nc.tensor.transpose(bank[0:rows, t * P:(t + 1) * P], src(n, t), ident[:, :])
                    ins.then_inc(turned, 1)

            def out_turns(l, name, buf):
                for f in range(buf.shape[-1] // P):
                    bank = turn_bank(l, name, 0, f)
                    for i in range(NT):
                        ins = nc.tensor.transpose(bank[:, i * P:(i + 1) * P], buf[:, i, f * P:(f + 1) * P], ident[:, :])
                    ins.then_inc(turned, 1)

            def attend(l, ps):
                kd = ps.kdim
                gate = f"gate{ps.filler}"

                def gate_terms(l, p, n0, n1):
                    if ps.filler is not None:
                        for k in range(2):
                            a, b = max(n0 - 24 * k, 0), min(n1 - 24 * k, 24)
                            if a < b:
                                unit_terms(l, gate, k, p, a, b, h_rhs)

                def body(p, kv):
                    hd = l * NHD + HB[ps.name] + 2 * p
                    st = l * (4 * NHD) + 4 * HB[ps.name] + 8 * p

                    def score(s):
                        e, i = divmod(s, NT)
                        k0, w = ps.keys(i)
                        if i == 0:
                            pe.wait_ge(qk_ready, hd + (e + 1))
                            if ps is FOX:
                                pe.wait_ge(cum_in[e], l * (16 * H) + p * 32 + 32)
                        pe.wait_ge(biased, st + (s + 1))
                        q = [t[0:kd, e, i * P:(i + 1) * P] for t in (q_hi, q_lo)]
                        k = [t[0:kd, e, k0:k0 + w] for t in (k_hi, k_lo)]
                        for n in range(3):
                            product(scores[s % 2][:, 0:w], q, k, n, 3, scored)

                    def turn_probs(s):
                        n, w = ps.tiles(s % NT)
                        pe.wait_ge(exped, st + (s + 1))
                        bank = turn_bank(l, ps.name, 8 * p, s)
                        for t in range(n):
                            ins = nc.tensor.transpose(bank[0:w, t * P:(t + 1) * P],
                                                      work[:, s % 2, t * w:(t + 1) * w], ident[:, :])
                        ins.then_inc(turned, 1)

                    def apply(s):
                        e, i = divmod(s, NT)
                        n, w = ps.tiles(i)
                        t0 = ps.keys(i)[0] // P
                        if i == 0:
                            pe.wait_ge(head_done, hd + (e + 1))
                        split_at = l * NTN + 8 * p + (TB[ps.name] + s + 3)
                        if w < P:
                            wait_apart(pe, turn_ready, split_at)
                        else:
                            pe.wait_ge(turn_ready, split_at)
                        for t in range(n):
                            probs = [x_[0:w, s % 2, t * P:(t + 1) * P] for x_ in (p_hi, p_lo)]
                            vals = [x_[0:w, t0 + t, bass.ds(kv(e) * HD, HD)] for x_ in (v_hi, v_lo)]
                            for m in range(3):
                                product(o_acc[e][:, i * HD:(i + 1) * HD], probs, vals, 3 * t + m, 3 * n, applied)

                    gate_terms(l, p, 0, 16)
                    score(0)
                    for s in range(8):
                        if s < 7:
                            score(s + 1)
                        gate_terms(l, p, 16 + 4 * s, 20 + 4 * s)
                        turn_probs(s)
                        if s > 0:
                            apply(s - 1)
                    apply(7)
                pairs(pe, ps, body)

            def branch(l, b):
                wait_apart(pe, turn_ready, l * NTN + (TB["y_" + ("nsa", "swa", "mla", "fox")[b]] + BW // P + 2))
                units(pe, f"br{b}", lambda k, j: whole_unit(l, f"br{b}", k, j, y_rhs))

            def project(l, name, rhs=h_rhs, first=0, count=None, free=S):
                units(pe, name, lambda k, j: whole_unit(l, name, k, j, rhs, free), first, count)

            def wait_split(l, name, n):
                wait_apart(pe, split_ready, l * NSP + SPB[name] + n)

            pe.wait_ge(s_const, 7)
            pe.wait_ge(s_rows, 16 * (2 * len(GAINS) + KVH + 4))
            nc.tensor.transpose(turn[0][:, 0:L * NG], gain_rows[:, :], ident[0:L * NG, 0:L * NG])
            nc.tensor.transpose(turn[0][:, P:P + L * 2 * CMP_LEN], pe_rows[:, :], ident[:, :]).then_inc(s_pe, 1)
            pe.wait_ge(s_dve, 1)
            nc.tensor.matmul(scores[0][0:R_END, :], inv_row[:, :], pos_row[0:1, 0:S], start=True,
                             stop=True).then_inc(s_angle, 1)
            pe.wait_ge(s_in, 32)
            for c in range(KT):
                if c == 1:
                    pe.wait_ge(s_dve, 3)
                if c >= 2:
                    pe.wait_ge(s_act, c - 1)
                for t in range(NT):
                    ins = nc.tensor.transpose(turn[(c + 1) % 2][:, t * P:(t + 1) * P], x_tok[:, t, c * P:(c + 1) * P],
                                              ident[:, :])
                ins.then_inc(s_pe, 1)
            pe.wait_ge(s_mem, 3 + MT)
            for c in range(KT):
                if c >= 2:
                    pe.wait_ge(s_mem, 3 + MT + c - 1)
                for t in range(MT):
                    ins = nc.tensor.transpose(o_acc[c % 2][:, t * P:(t + 1) * P], mem_in[:, t, c * P:(c + 1) * P],
                                              ident[:, :])
                ins.then_inc(s_mem_turned, 1)
            pe.wait_ge(s_act, KT)
            pe.wait_ge(s_dve, 4)

            with pe.Fori(0, L) as l:
                norm(l, "mix_pre")
                wait_split(l, "mix_pre", KT)
                project(l, "misc")
                project(l, "nsa")
                wait_chunk_read(pe, l, "misc", 0)
                g = slice(R_G, R_G + 3 * H)
                for t in range(NT):
                    ins = nc.tensor.transpose(SUMS[:, t * 3 * H:(t + 1) * 3 * H], narrow[g, t * P:(t + 1) * P],
                                              ident[g, g])
                ins.then_inc(ng_turned, 1)
                for cv in range(2):
                    c = CB["cmp"] + cv
                    pe.wait_ge(blocks_in, l * 64 + 32 * (cv + 1))
                    if cv == 0:
                        pe.wait_ge(blocks_zero, l * 2 + 2)
                    pe.wait_ge(blocks_tok, l * 6 + 3 * (cv + 1))
                    pe.wait_ge(acc_free[c % 2], free_at(l, c, 1, 0))
                    for n in range(CMP_LEN):
                        ins = nc.tensor.matmul(acc[c % 2][:, 0:NCP], block_w[:, n, :], block_in[:, n, :],
                                               start=(n == 0), stop=(n == CMP_LEN - 1))
                    ins.then_inc(part_ready, 1)
                wait_chunk_read(pe, l, "cmp", 1)
                bank = turn_bank(l, "v_cmp", 0, 0)
                nc.tensor.transpose(bank[0:NCP, 0:P], vc_feat, ident[:, :]).then_inc(turned, 1)
                wait_apart(pe, ng_tanh, l + 1)
                attend(l, CMP)
                value_turns(l, "v_sel", 1, lambda n, t: proj[:, PJ_V["sel"], t * P:(t + 1) * P])
                attend(l, SEL)
                value_turns(l, "v_win", 1, lambda n, t: proj[:, PJ_V["win"], t * P:(t + 1) * P])
                attend(l, WIN)
                pe.wait_ge(head_done, l * NHD + HB["swa"] + 2)
                out_turns(l, "y_nsa", y_tok)
                branch(l, 0)
                project(l, "swa")
                wait_chunk_read(pe, l, "swa", 5)
                value_turns(l, "v_swa", 1, lambda n, t: proj[:, PJ_V["swa"], t * P:(t + 1) * P])
                attend(l, SWA)
                pe.wait_ge(head_done, l * NHD + HB["mla"] + 2)
                out_turns(l, "y_swa", y_tok)
                branch(l, 1)
                project(l, "mla")
                norm(l, "mlaq")
                norm(l, "mlakv")
                wait_split(l, "mlaq", 2)
                project(l, "qup", y_rhs)
                wait_split(l, "mlakv", 1)
                project(l, "kvup", lambda kt: (y_hi[:, 2, :], y_lo[:, 2, :]))
                wait_chunk_read(pe, l, "kvup", 7)
                for n in range(4):
                    bank = turn_bank(l, "v_mla", 0, n)
                    for t in range(NT):
                        for e in range(2):
                            ins = nc.tensor.transpose(bank[:, t * P + e * HD:t * P + (e + 1) * HD],
                                                      proj[HD:P, PJ_KV + 2 * n + e, t * P:(t + 1) * P],
                                                      ident[HD:P, HD:P])
                    ins.then_inc(turned, 1)
                attend(l, MLA)
                pe.wait_ge(head_done, l * NHD + HB["fox"] + 2)
                out_turns(l, "y_mla", y_tok)
                branch(l, 2)
                project(l, "fox")
                wait_chunk_read(pe, l, "fox", 11)
                value_turns(l, "v_fox", 4, lambda n, t: proj[:, PJ_V["fox"] + n, t * P:(t + 1) * P])
                attend(l, FOX)
                pe.wait_ge(head_done, l * NHD + HB["xa"] + 2)
                out_turns(l, "y_fox", y_tok)
                branch(l, 3)
                wait_split(l, "merged", KT)
                for c in range(KT):
                    whole_unit(l, "wout", c, 0, h_rhs)
                    if c > 0:
                        sum_squares(l, "mix_post", c - 1, KT)
                sum_squares(l, "mix_post", KT - 1, KT)
                spread_rstd(l, "mix_post")
                norm(l, "xa_pre")
                wait_split(l, "xa_pre", KT)
                project(l, "xq")
                wait_split(l, "mem", KT)
                project(l, "xkv", lambda kt: (m_hi[:, kt, :], m_lo[:, kt, :]), free=M)
                wait_chunk_read(pe, l, "xkv", 3)
                value_turns(l, "v_xa", 2, lambda n, t: proj_x[:, PJ_V["xa"] + n, t * P:(t + 1) * P], tiles=MT)
                attend(l, XA)
                pe.wait_ge(head_done, l * NHD + NHD + 2)
                out_turns(l, "y_xa", y_tok_x)
                pe.wait_ge(turn_ready, l * NTN + NTN + 2)
                for c in range(KT):
                    unit_terms(l, "xo", c // 4, 0, 6 * (c % 4), 6 * (c % 4) + 6, y_rhs)
                    if c > 0:
                        sum_squares(l, "xa_post", c - 1, KT)
                sum_squares(l, "xa_post", KT - 1, KT)
                spread_rstd(l, "xa_post")
                norm(l, "ffn_pre")
                wait_split(l, "ffn_pre", KT)
                project(l, "ffin")
                for c in range(KT):
                    ch = CB["ffout"] + c
                    n = kt0 = 0
                    pe.wait_ge(acc_free[ch % 2], free_at(l, ch, 1, 0))
                    for k, kts in enumerate(FF_UNITS):
                        u = UB["ffout"] + 3 * c + k
                        pe.wait_ge(w_ready, unit_at(l, u, 0) + 3)
                        for kt in range(kts):
                            if c == 0:
                                pe.wait_ge(split_ready, l * NSP + (SPB["ffa"] + kt0 + kt + 1))
                            for m in range(3):
                                ins = product(acc[ch % 2][:, :], weights(u, kts, P, kt, 0, P),
                                              (a_hi[:, kt0 + kt, :], a_lo[:, kt0 + kt, :]), n, 3 * FK)
                                n += 1
                        ins.then_inc(w_used, 1)
                        kt0 += kts
                    if c > 0:
                        sum_squares(l, "ffn_post", c - 1, KT)
                sum_squares(l, "ffn_post", KT - 1, KT)
                spread_rstd(l, "ffn_post")

            pe.wait_ge(trunk_new, L * NRS)
            for n in range(2 * NT):
                t, half = divmod(n, 2)
                if n >= 2:
                    pe.wait_ge(s_act, KT + n - 1)
                for c in range(NT):
                    ins = nc.tensor.transpose(turn[n % 2][:, c * P:(c + 1) * P],
                                              trunk[:, half * NT + c, t * P:(t + 1) * P], ident[:, :])
                ins.then_inc(s_pe, 1)

        @block.vector
        def _(dve):
            dve.sem_inc(w_ready, CREDIT)
            dve.sem_inc(acc_free[0], 1)
            dve.sem_inc(acc_free[1], 1)
            dve.sem_inc(biased, CREDIT)
            dve.sem_inc(turn_ready, CREDIT)
            dve.sem_inc(head_done, CREDIT)

            def split_rest(l, u, j):
                dve.wait_ge(w_high, unit_at(l, u, j) + 1)
                nc.vector.tensor_tensor(w_lo[:, u % 2, :], w_f32[:, u % 2, :], w_hi[:, u % 2, :].bitcast(F32),
                                        ALU.subtract).then_inc(w_ready, 1)

            def next_unit(l, name, k, j):
                split_rest(l, UB[name] + k + 1, j)

            def gain(l, name, c):
                return gains[:, bass.ds(l * NG + (GB[name] + c), 1)]

            def rstd_rows(l, name, width):
                n = dict(NORMS)[name]
                dve.wait_ge(summed, l * NSQ + (SQB[name] + n + 2))
                nc.vector.tensor_scalar(mean_sq[:, :], SUMS[:, 0:NT], 1.0 / width, EPS, ALU.mult,
                                        ALU.add).then_inc(ms_ready, 1)
                dve.wait_ge(rstd_ready, l * NNORM + NB_OF[name] + 1)
                nc.vector.tensor_tensor(diag.rearrange("p (t c) -> p t c", t=NT),
                                        ident[:, :].unsqueeze(1).to_broadcast([P, NT, P]),
                                        rstd[:, :].unsqueeze(2).to_broadcast([P, NT, P]), ALU.mult).then_inc(diag_ready, 1)
                dve.wait_ge(rbc_ready, l * NNORM + NB_OF[name] + 1)

            def rest_of_chunk(l, name, c, dst, src, high):
                dve.wait_ge(split_high, l * NSP + (SPB[name] + c + 1))
                nc.vector.tensor_tensor(dst, src, high.bitcast(F32), ALU.subtract).then_inc(split_ready, 1)

            def norm(l, name, width, src, hi, lo):
                n = dict(NORMS)[name]
                rstd_rows(l, name, width)
                for c in range(n + 1):
                    if c < n:
                        if c > 1:
                            dve.wait_ge(split_ready, l * NSP + (SPB[name] + c - 1))
                        nc.vector.scalar_tensor_tensor(work[:, c % 2, :], src(c), gain(l, name, c), RBC[:, :], ALU.mult,
                                                       ALU.mult).then_inc(split_in, 1)
                    if c > 0:
                        rest_of_chunk(l, name, c - 1, lo(c - 1), work[:, (c - 1) % 2, :], hi(c - 1))

            def h_norm(l, name):
                norm(l, name, D, lambda c: trunk[:, c, :], lambda c: h_hi[:, c, :], lambda c: h_lo[:, c, :])

            def add_to_trunk(l, name, phase):
                rstd_rows(l, name, D)
                wait_chunk_read(dve, l, phase, KT - 1)
                for c in range(KT + 1):
                    at = l * NRS + (RB[name] + c)
                    if c < KT:
                        if c > 1:
                            dve.wait_ge(trunk_new, at - 1)
                        nc.vector.scalar_tensor_tensor(work[:, c % 2, :], wide[:, c, :], gain(l, name, c), RBC[:, :],
                                                       ALU.mult, ALU.mult).then_inc(scaled_out, 1)
                    if c > 0:
                        dve.wait_ge(scaled_out, at)
                        nc.vector.tensor_tensor(trunk[:, c - 1, :], trunk[:, c - 1, :], work[:, (c - 1) % 2, :],
                                                ALU.add).then_inc(trunk_new, 1)

            def turn_rest(l, name, n, k, dst, bank, high):
                t = l * NTN + n + (TB[name] + k)
                dve.wait_ge(turn_high, t + 1)
                nc.vector.tensor_tensor(dst, bank, high.bitcast(F32), ALU.subtract).then_inc(turn_ready, 1)

            def value_turns(l, name, count, rows, tiles):
                for n in range(count):
                    bank = turn[(TB[name] + n) % 2][0:rows, 0:tiles * P].rearrange("p (t f) -> p t f", t=tiles)
                    at = (slice(0, rows), slice(0, tiles), slice(n * P, (n + 1) * P))
                    turn_rest(l, name, 0, n, v_lo[at], bank, v_hi[at])

            def out_turns(l, name, count):
                for f in range(count):
                    turn_rest(l, name, 0, f, y_lo[:, f, :], turn[(TB[name] + f) % 2][:, :], y_hi[:, f, :])

            def group_keys(l, n, chunk):
                for kv in range(KVH):
                    ins = nc.vector.tensor_copy(kg32[:, kv, :], proj[kv * HD:(kv + 1) * HD, chunk, :])
                ins.then_inc(kg_ready, 1)

            def attend(l, ps, kg=0):
                kd = ps.kdim
                keys = {"cmp": NCP, "xa": M}.get(ps.name, S)
                buf = proj_x if ps is XA else proj
                y = y_tok_x if ps is XA else y_tok
                steps = 4 if ps.add else 3

                def body(p, kv):
                    hd = l * NHD + HB[ps.name] + 2 * p
                    st = l * (4 * NHD) + 4 * HB[ps.name] + 8 * p

                    def stage(e):
                        dve.wait_ge(scored, 4 * hd + (4 * e + 4))
                        if e == 1:
                            dve.wait_ge(qk_ready, hd + 1)
                        if ps.grouped:
                            if ps is CMP:
                                wait_chunk_read(dve, l, "cmp", 0)
                            else:
                                dve.wait_ge(kg_ready, l * 3 + (kg + 1))
                            k_src = k_in = kg32[:, bass.ds(kv(e), 1), 0:keys]
                        elif ps is MLA:
                            k_src = k_in = proj[0:HD, bass.ds(2 * p + (PJ_KV + e), 1), :]
                        else:
                            k_in, k_src = buf[e * HD:(e + 1) * HD, bass.ds(p + PJ_K[ps.name], 1), 0:keys], k32[:, 0:keys]
                            nc.vector.tensor_copy(k_src, k_in)
                        if ps is MLA:
                            q_src = proj[0:kd, bass.ds(2 * p + e, 1), :]
                        else:
                            q_src = q32[:, :]
                            s = q_scale[e * HD:(e + 1) * HD, bass.ds(2 * p + e, 1)] if ps.slopes else -(HD ** -0.5)
                            nc.vector.tensor_scalar(q_src, buf[e * HD:(e + 1) * HD, bass.ds(p, 1), :], s, None, ALU.mult)
                        if ps.slopes:
                            table, first = (head_sink, l * H) if ps.sink else (head_plain, 0)
                            nc.vector.tensor_copy(head_now[:, e, :], table[:, bass.ds(2 * p + e + first, 1), :])
                        nc.vector.tensor_copy(k_hi[0:HD, e, 0:keys], k_in).then_inc(staged, 1)
                        dve.wait_ge(staged, hd + (e + 1))
                        nc.vector.tensor_tensor(k_lo[0:HD, e, 0:keys], k_src, k_hi[0:HD, e, 0:keys].bitcast(F32),
                                                ALU.subtract)
                        rows = kd if ps is MLA else HD
                        dve.wait_ge(q_high, hd + (e + 1))
                        nc.vector.tensor_tensor(q_lo[0:rows, e, :], q_src, q_hi[0:rows, e, :].bitcast(F32),
                                                ALU.subtract).then_inc(qk_ready, 1)

                    def head_out(e):
                        at = l * NMS + steps * 2 * p + (NSB[ps.name] + steps * e)
                        dve.wait_ge(applied, st + (4 * e + 6))
                        if ps.sink:
                            dve.wait_ge(sink_ready, l * H + 2 * p + (e + 1))
                        nc.vector.tensor_tensor(norm4[:, e, 0, :], row_sum[:, e, :], sink_exp[:, e, :] if ps.sink else ZERO4,
                                                ALU.add).then_inc(normed, 1)
                        dve.wait_ge(normed, at + 1)
                        nc.vector.reciprocal(norm4[:, e, 1, :], norm4[:, e, 0, :]).then_inc(normed, 1)
                        dve.wait_ge(normed, at + 2)
                        if ps.gate is not None:
                            dve.wait_ge(ng_coef, l * 2 + 2)
                        g = 3 if ps.gate is None else ps.gate
                        nc.vector.tensor_tensor(norm4[:, e, 2, :], norm4[:, e, 1, :], coef[:, g, :, bass.ds(2 * p + e, 1)],
                                                ALU.mult).then_inc(normed, 1)
                        dve.wait_ge(normed, at + 3)
                        o = o_acc[e][:, 0:NT * HD].rearrange("p (t d) -> p t d", t=NT)
                        c = norm4[:, e, 2, :].unsqueeze(2).to_broadcast([P, NT, HD])
                        dst = y[:, :, bass.ds((2 * p + e) * HD, HD)]
                        if ps.add:
                            tmp = squares[:, 1, 0:NT * HD].rearrange("p (t d) -> p t d", t=NT)
                            nc.vector.tensor_tensor(tmp, o, c, ALU.mult).then_inc(normed, 1)
                            dve.wait_ge(normed, at + 4)
                            nc.vector.tensor_tensor(dst, dst, tmp, ALU.add).then_inc(head_done, 1)
                        else:
                            nc.vector.tensor_tensor(dst, o, c, ALU.mult).then_inc(head_done, 1)

                    stage(0)
                    if ps.filler is not None:
                        next_unit(l, f"gate{ps.filler}", 0, p)
                    stage(1)
                    for s in range(9):
                        if s < 8:
                            e, i = divmod(s, NT)
                            w = ps.keys(i)[1]
                            dve.wait_ge(turned, l * NTN + 8 * p + (TB[ps.name] + s + 1))
                            due = dve.to_reg(st + (s + 9))
                            dve.wait_ge(s_masked, 3 * NT)
                            dve.wait_ge(scored, due)
                            nc.vector.tensor_tensor_reduce(
                                work[:, s % 2, 0:w], scores[s % 2][:, 0:w], bias(ps, i),
                                head_now[:, e, 0:1] if ps.slopes else 1.0, head_now[:, e, 1:2] if ps.sink else NO_SINK,
                                ALU.add, ALU.min, neg_max[:, e, i:i + 1]).then_inc(biased, 1)
                        if s == 4 and ps.filler is not None:
                            next_unit(l, f"gate{ps.filler}", 1, p)
                        if s > 0:
                            t = s - 1
                            n, rows = ps.tiles(t % NT)
                            turn_rest(l, ps.name, 8 * p, t, p_lo[0:rows, t % 2, 0:n * P],
                                      turn[(TB[ps.name] + t) % 2][0:rows, 0:n * P], p_hi[0:rows, t % 2, 0:n * P])
                        if s == 6:
                            head_out(0)
                    head_out(1)
                pairs(dve, ps, body)

            def branch(l, b):
                def body(k, j):
                    next_unit(l, f"br{b}", k, j)
                    for n in range(2):
                        c = CB[f"br{b}"] + 2 * k + n
                        i = 4 * j + 2 * k + n
                        wait_chunk(dve, l, f"br{b}", k, j, n)
                        if b == 0:
                            dve.wait_ge(x_saved, l * 16 + 16)
                            dst = trunk[:, bass.ds(i, 1), :]
                        else:
                            dst = work[:, n, :]
                        nc.vector.scalar_tensor_tensor(dst, wide[:, bass.ds(i, 1), :], 1.0, acc[c % 2][:, :], ALU.add,
                                                       ALU.mult).then_inc(acc_free[c % 2], 1)
                        if b > 0:
                            dve.wait_ge(acc_free[c % 2], free_at(l, c, 2, j) + 1)
                            m = trunk[:, bass.ds(i, 1), :]
                            nc.vector.tensor_tensor(m, m, dst, ALU.add).then_inc(merged, 1)
                units(dve, f"br{b}", body)

            def project(l, name):
                units(dve, name, lambda k, j: next_unit(l, name, k, j))

            def rotate(l, n, rows_of):
                at = l * 36 + 4 * n
                r = slice(R_R, R_END)
                half = ROT // 2
                wait_apart(dve, rope, at)
                nc.vector.stream_shuffle(work[r, 0, :], rows_of, list(range(half, ROT)) + list(range(half))).then_inc(rope, 1)
                nc.vector.tensor_tensor(work[r, 1, :], rows_of, cos[r, :], ALU.mult).then_inc(rope, 1)
                dve.wait_ge(rope, at + 1)
                nc.vector.tensor_tensor(work[r, 0, :], work[r, 0, :], sin[r, :], ALU.mult).then_inc(rope, 1)
                dve.wait_ge(rope, at + 3)
                nc.vector.tensor_tensor(rows_of, work[r, 0, :], work[r, 1, :], ALU.add).then_inc(rope, 1)

            dve.wait_ge(s_rows, 16 * (2 * len(GAINS) + KVH + 4))
            nc.vector.tensor_copy(pos_row[:, :], pos_int[:, :]).then_inc(s_dve, 1)
            dve.wait_ge(s_pe, 1)
            nc.vector.tensor_copy(gains[:, :], turn[0][:, 0:L * NG]).then_inc(s_dve, 1)
            nc.vector.tensor_copy(cmp_pe[:, :], turn[0][:, P:P + L * 2 * CMP_LEN]).then_inc(s_dve, 1)
            dve.wait_ge(s_angle, 1)
            r = slice(R_R, R_END)
            nc.vector.tensor_copy(ang[r, 0, :], scores[0][r, :]).then_inc(s_dve, 1)
            dve.wait_ge(s_const, 7)
            nc.vector.tensor_scalar(head_sink[:, :, 1], head_sink[:, :, 2], -1.0, None, ALU.mult)
            for i in range(NT):
                w = (i + 1) * P
                pc = pos_row[:, S + i:S + i + 1]
                far, far_cmp = dist[:, off(i):off(i) + w], dist_cmp[:, i, 0:NC]
                nc.vector.tensor_scalar(far, pos_row[:, 0:w], pc, None, ALU.subtract).then_inc(s_far, 1)
                nc.vector.tensor_scalar(far_cmp, pos_row[:, CMP_LEN - 1:S:CMP_STRIDE], pc, None,
                                        ALU.subtract).then_inc(s_far, 1)
                dve.wait_ge(s_far, 2 * i + 1)
                nc.vector.scalar_tensor_tensor(far, far, -1.0, far, ALU.mult, ALU.max).then_inc(s_dist, 1)
                dve.wait_ge(s_far, 2 * i + 2)
                nc.vector.scalar_tensor_tensor(far_cmp, far_cmp, -1.0, far_cmp, ALU.mult, ALU.max).then_inc(s_dist, 1)
            dve.wait_ge(s_in, 32)
            for t in range(MT):
                if t > 0:
                    dve.wait_ge(s_mem, t)
                nc.vector.tensor_tensor_reduce(squares[:, :, :].rearrange("p a b -> p (a b)"), mem_in[:, t, :],
                                               mem_in[:, t, :], 1.0, 0.0, ALU.mult, ALU.add,
                                               mem_ms[:, 0, t:t + 1]).then_inc(s_mem, 1)
            dve.wait_ge(s_mem, 2)
            nc.vector.tensor_scalar(mem_ms[:, 1, :], mem_ms[:, 0, :], 1.0 / D, EPS, ALU.mult, ALU.add).then_inc(s_mem, 1)
            dve.wait_ge(s_mem_rstd, 1)
            for t in range(MT):
                nc.vector.tensor_scalar(mem_in[:, t, :], mem_in[:, t, :], mem_ms[:, 2, t:t + 1], None,
                                        ALU.mult).then_inc(s_mem, 1)
            for c in range(KT):
                dve.wait_ge(s_mem_turned, c + 1)
                nc.vector.tensor_copy(mem_t[:, c, :], o_acc[c % 2][:, 0:M]).then_inc(s_mem, 1)
            a, t = ang[r, 0, :], ang[r, 1, :]
            n = 4
            for many in (4096.0, 1.0):
                dve.wait_ge(s_dve, n)
                nc.vector.tensor_scalar(t, a, 1.0 / (TWO_PI * many), MAGIC, ALU.mult, ALU.add).then_inc(s_dve, 1)
                dve.wait_ge(s_dve, n + 1)
                nc.vector.tensor_scalar(t, t, MAGIC, None, ALU.subtract).then_inc(s_dve, 1)
                n += 2
                for part in two_pi_parts():
                    dve.wait_ge(s_dve, n)
                    nc.vector.scalar_tensor_tensor(a, t, -part * many, a, ALU.mult, ALU.add).then_inc(s_dve, 1)
                    n += 1
            dve.wait_ge(s_dve, n)
            nc.vector.tensor_scalar(a, a, 3.1415925, -3.1415925, ALU.min, ALU.max).then_inc(s_dve, 1)
            dve.wait_ge(s_dve, n + 1)
            nc.vector.scalar_tensor_tensor(t, a, -1.0, a, ALU.mult, ALU.max).then_inc(s_dve, 1)
            dve.wait_ge(s_dve, n + 2)
            nc.vector.tensor_scalar(t, t, -1.0, math.pi / 2, ALU.mult, ALU.add).then_inc(s_reduced, 1)

            with dve.Fori(0, L) as l:
                split_rest(l, 0, 0)
                h_norm(l, "mix_pre")
                project(l, "misc")
                project(l, "nsa")
                nc.vector.memset(kg32[:, :, NC:NCP], 0.0)
                nc.vector.memset(vc_feat[:, NC:NCP], 0.0)
                for cv in range(2):
                    wait_chunk_read(dve, l, "nsa", 9)
                    if cv == 1:
                        dve.wait_ge(part_ready, l * NPT + 1)
                    src = proj[:, PJ_K["cmp"] + cv, :]
                    for n in range(2):
                        nc.vector.tensor_copy(block_in[:, n * CMP_STRIDE:(n + 1) * CMP_STRIDE, 0:NC],
                                              src[:, n * CMP_STRIDE:n * CMP_STRIDE + NC * CMP_STRIDE].rearrange(
                                                  "p (c n) -> p n c", n=CMP_STRIDE)).then_inc(blocks_tok, 1)
                    nc.vector.tensor_copy(block_in[:, :, NC],
                                          cmp_pe[:, bass.ds(l * (2 * CMP_LEN) + cv * CMP_LEN, CMP_LEN)]).then_inc(blocks_tok, 1)
                    c = CB["cmp"] + cv
                    dve.wait_ge(part_ready, l * NPT + (cv + 1))
                    if cv == 0:
                        for kv in range(KVH):
                            g = slice(kv * HD, (kv + 1) * HD)
                            ins = nc.vector.tensor_scalar(kg32[:, kv, 0:NC], acc[c % 2][g, 0:NC], acc[c % 2][g, NC:NCP],
                                                          None, ALU.add)
                        ins.then_inc(acc_free[c % 2], 1)
                    else:
                        nc.vector.tensor_scalar(vc_feat[:, 0:NC], acc[c % 2][:, 0:NC], acc[c % 2][:, NC:NCP], None,
                                                ALU.add).then_inc(acc_free[c % 2], 1)
                dve.wait_ge(ng_tanh, l + 1)
                for h in range(3):
                    ins = nc.vector.tensor_scalar(coef[:, h, :, :], gate_tanh[:, :, h:3 * H:3], 0.5, 0.5, ALU.mult, ALU.add)
                ins.then_inc(ng_coef, 1)
                dve.wait_ge(ng_coef, l * 2 + 1)
                nc.vector.tensor_tensor(coef[:, 0, :, :], coef[:, 0, :, :],
                                        row_sees[:, :].unsqueeze(2).to_broadcast([P, NT, H]), ALU.mult).then_inc(ng_coef, 1)
                value_turns(l, "v_cmp", 1, NCP, 1)
                attend(l, CMP)
                group_keys(l, 0, PJ_K["sel"])
                value_turns(l, "v_sel", 1, P, NT)
                attend(l, SEL, 0)
                group_keys(l, 1, PJ_K["win"])
                value_turns(l, "v_win", 1, P, NT)
                attend(l, WIN, 1)
                out_turns(l, "y_nsa", BW // P)
                branch(l, 0)
                project(l, "swa")
                wait_chunk_read(dve, l, "swa", 5)
                group_keys(l, 2, PJ_K["swa"])
                value_turns(l, "v_swa", 1, P, NT)
                attend(l, SWA, 2)
                out_turns(l, "y_swa", BW // P)
                branch(l, 1)
                project(l, "mla")
                wait_chunk_read(dve, l, "mla", 2)
                norm(l, "mlaq", QR, lambda c: proj[:, PJ_CQ + c, :], lambda c: y_hi[:, c, :], lambda c: y_lo[:, c, :])
                norm(l, "mlakv", KVR, lambda c: proj[:, PJ_CQ + 2, :], lambda c: y_hi[:, 2, :], lambda c: y_lo[:, 2, :])
                project(l, "qup")
                project(l, "kvup")
                rotate(l, 0, narrow[r, :])
                wait_chunk_read(dve, l, "qup", 7)
                for h in range(H):
                    rotate(l, 1 + h, proj[r, h, :])
                for e in range(2):
                    dve.wait_ge(rot_high, l * 2 + (e + 1))
                    dve.wait_ge(rope, l * 36 + 36)
                    nc.vector.tensor_tensor(k_lo[HD:HD + ROT, e, :], narrow[r, :], k_hi[HD:HD + ROT, e, :].bitcast(F32),
                                            ALU.subtract)
                value_turns(l, "v_mla", 4, P, NT)
                attend(l, MLA)
                out_turns(l, "y_mla", BW // P)
                branch(l, 2)
                project(l, "fox")
                at = l * 8
                nc.vector.tensor_scalar(cum, narrow[R_F:R_F + H, :], f_bias[:, bass.ds(l, 1)], None,
                                        ALU.add).then_inc(forget, 1)
                dve.wait_ge(forget, at + 1)
                nc.vector.scalar_tensor_tensor(logit, cum, -1.0, cum, ALU.mult, ALU.max).then_inc(forget, 1)
                dve.wait_ge(forget, at + 2)
                nc.vector.tensor_scalar(cum, cum, 0.0, None, ALU.min).then_inc(forget, 1)
                dve.wait_ge(forget_act, l * 2 + 2)
                dve.wait_ge(forget, at + 3)
                nc.vector.tensor_tensor(logit, cum, cum_lo, ALU.subtract).then_inc(forget, 1)
                dve.wait_ge(forget, at + 4)
                nc.vector.tensor_tensor_scan(cum, logit, logit, 0.0, ALU.add, ALU.bypass).then_inc(forget, 1)
                dve.wait_ge(forget, at + 5)
                nc.vector.tensor_copy(cum_hi.bitcast(F32R), cum).then_inc(forget, 1)
                dve.wait_ge(forget, at + 6)
                nc.vector.tensor_tensor(cum_lo.bitcast(F32R), cum, cum_hi, ALU.subtract).then_inc(forget, 1)
                nc.vector.memset(q_lo[HD:HD + 1, :, :].bitcast(F32), 0.0)
                nc.vector.memset(q_hi[HD:HD + 1, :, :].bitcast(F32), 1.0).then_inc(forget, 1)
                value_turns(l, "v_fox", 4, P, NT)
                attend(l, FOX)
                out_turns(l, "y_fox", BW // P)
                branch(l, 3)
                for c in range(KT):
                    rest_of_chunk(l, "merged", c, h_lo[:, c, :], trunk[:, c, :], h_hi[:, c, :])
                project(l, "wout")
                dve.wait_ge(x_back, l * 16 + 16)
                add_to_trunk(l, "mix_post", "wout")
                h_norm(l, "xa_pre")
                dve.wait_ge(mem_back, l * 16 + 16)
                for c in range(KT + 1):
                    if c < KT:
                        dve.wait_ge(split_ready, l * NSP + (SPB["mem"] + c - 1))
                        nc.vector.tensor_scalar(work[:, c % 2, 0:M], m_f32[:, c, :], gain(l, "mem", c), None,
                                                ALU.mult).then_inc(split_in, 1)
                    if c > 0:
                        rest_of_chunk(l, "mem", c - 1, m_lo[:, c - 1, :], work[:, (c - 1) % 2, 0:M], m_hi[:, c - 1, :])
                project(l, "xq")
                project(l, "xkv")
                wait_chunk_read(dve, l, "xkv", 3)
                value_turns(l, "v_xa", 2, P, MT)
                attend(l, XA)
                out_turns(l, "y_xa", XH * HD // P)
                project(l, "xo")
                add_to_trunk(l, "xa_post", "xo")
                h_norm(l, "ffn_pre")

                def ff(j):
                    c = CB["ffin"]
                    next_unit(l, "ffin", 0, j)
                    dve.wait_ge(ff_tanh, l * FK + j + 1)
                    nc.vector.scalar_tensor_tensor(work[:, 0, :], work[:, 0, :], 1.0, acc[c % 2][:, :], ALU.add,
                                                   ALU.mult).then_inc(acc_free[c % 2], 1)
                    next_unit(l, "ffin", 1, j)
                    wait_chunk(dve, l, "ffin", 1, j, 0)
                    dve.wait_ge(acc_free[c % 2], free_at(l, c, 1, j) + 1)
                    nc.vector.scalar_tensor_tensor(work[:, 0, :], work[:, 0, :], 0.5, acc[(c + 1) % 2][:, :], ALU.mult,
                                                   ALU.mult).then_inc(acc_free[(c + 1) % 2], 1)
                    dve.wait_ge(split_high, l * NSP + j + (SPB["ffa"] + 1))
                    a = a_hi[:, bass.ds(j, 1), :]
                    nc.vector.tensor_tensor(a_lo[:, bass.ds(j, 1), :], work[:, 0, :], a.bitcast(F32),
                                            ALU.subtract).then_inc(split_ready, 1)
                with dve.Fori(0, FK) as j:
                    ff(j)
                for n in range(3 * KT - 1):
                    next_unit(l, "ffout", n, 0)
                add_to_trunk(l, "ffn_post", "ffout")


_INS = ["x", "mem", "positions", "mix_norm_pre", "w_in", "nsa_cmp_w", "nsa_cmp_pe", "swa_sinks", "mla_q_norm",
        "mla_w_q_up", "mla_kv_norm", "mla_w_kv_up", "fox_f_bias", "w_branch", "w_gate", "w_out", "mix_norm_post",
        "xa_norm_pre", "xa_mem_norm", "xa_w_q", "xa_w_kv", "xa_w_o", "xa_norm_post", "ffn_norm_pre", "ffn_w_in",
        "ffn_w_out", "ffn_norm_post"]


def kernel(**inputs):
    import concourse.bacc as bacc
    from concourse.bass_utils import run_bass_kernel_spmd

    nc = bacc.Bacc("TRN2", target_bir_lowering=False, num_devices=1)
    arrays, args = {}, []
    for name in _INS:
        a = np.ascontiguousarray(inputs[name])
        arrays[f"in_{name}_dram"] = a
        args.append(nc.dram_tensor(f"in_{name}_dram", a.shape, mybir.dt.from_np(a.dtype), kind="ExternalInput").ap())
    args.append(nc.dram_tensor("out_dram", (1, S, D), F32, kind="ExternalOutput").ap())
    build(nc, *args)
    r = run_bass_kernel_spmd(nc, [arrays], core_ids=[0])
    return r.results[0]["out_dram"]
```

```python
import math
from contextlib import ExitStack

import concourse.bass as bass
import numpy as np
from concourse import mybir
from concourse.alu_op_type import AluOpType as ALU

F32 = mybir.dt.float32
F32R = mybir.dt.float32r
I32 = mybir.dt.int32
ACT = mybir.ActivationFunctionType

P = 128
S = 512
NT = S // P
D = 1024
KT = D // P
L = 2
M = 256
MT = M // P
EPS = 1e-6
HD = 64
H = 8
KVH = 2
XH = 4
CMP_LEN, CMP_STRIDE = 32, 16
NC = (S - CMP_LEN) // CMP_STRIDE + 1
NCP = NC + 1
WINDOW = 128
ROT = 32
QR, KVR = 256, 128
BW = 512
NB = 4
FF = ((8 * D + 3 * 256 - 1) // (3 * 256)) * 256
FK = FF // P
BIG = 1e30
NO_SINK = 3e38
CREDIT = 2

_cols = np.cumsum([0, 512, 128, 128, 128, 128, 128, 128, 24, 512, 128, 128, 256, 128, 32, 512, 512, 512, 8]).tolist()
(C_NQ, C_NKC, C_NVC, C_NKS, C_NVS, C_NKW, C_NVW, C_NG, C_SQ, C_SK, C_SV,
 C_MQ, C_MKV, C_MKR, C_FQ, C_FK, C_FV, C_FF, IN_COLS) = _cols
R_F, R_G, R_R = 0, 32, 64
R_END = R_R + ROT


def offsets(parts):
    at, out = 0, {}
    for name, n in parts:
        out[name] = at
        at += n
    return out, at


UNITS = [("misc", 1), ("nsa", 10), ("gate0", 8), ("br0", 4), ("swa", 6), ("gate1", 8), ("br1", 4), ("mla", 3),
         ("qup", 2), ("kvup", 2), ("gate2", 8), ("br2", 4), ("fox", 12), ("gate3", 8), ("br3", 4), ("wout", 8),
         ("xq", 2), ("xkv", 4), ("xo", 2), ("ffin", 2 * FK), ("ffout", 3 * KT)]
UB, NU = offsets(UNITS)
CHUNKS = [("misc", 1), ("nsa", 10), ("cmp", 2), ("gate0", 8), ("br0", 8), ("swa", 6), ("gate1", 8), ("br1", 8),
          ("mla", 3), ("qup", 8), ("kvup", 8), ("gate2", 8), ("br2", 8), ("fox", 12), ("gate3", 8), ("br3", 8),
          ("wout", 8), ("xq", 2), ("xkv", 4), ("xo", 8), ("ffin", 2 * FK), ("ffout", KT)]
CB, NCH = offsets(CHUNKS)
PASSES = [("cmp", 8), ("sel", 8), ("win", 8), ("swa", 8), ("mla", 8), ("fox", 8), ("xa", XH)]
HB, NHD = offsets(PASSES)
TURNS = [("v_cmp", 1), ("cmp", 32), ("v_sel", 1), ("sel", 32), ("v_win", 1), ("win", 32),
         ("v_swa", 1), ("swa", 32), ("v_mla", 4), ("mla", 32), ("v_fox", 4), ("fox", 32), ("v_xa", 2), ("xa", 16)]
TB, NTN = offsets(TURNS)
ITEMS = [("cmp", 4), ("sel", 4), ("win", 4), ("swa", 4), ("mla", 8), ("fox", 4), ("xa", 2)]
IB, NIT = offsets(ITEMS)
OUTS = [("nsa", 4), ("swa", 8), ("mla", 8), ("fox", 8), ("xa", XH)]
OB, NOUT = offsets(OUTS)
GROUPED = [("cmp", 1), ("sel", 1), ("win", 1), ("swa", 1)]
KGB, NKG = offsets(GROUPED)
NORMS = [("mix_pre", KT), ("mlaq", 2), ("mlakv", 1), ("mix_post", KT), ("xa_pre", KT), ("xa_post", KT),
         ("ffn_pre", KT), ("ffn_post", KT)]
SQB, NSQ = offsets(NORMS)
NB_OF = {name: i for i, (name, _) in enumerate(NORMS)}
NNORM = len(NORMS)
SPLITS = [("mix_pre", KT), ("mlaq", 2), ("mlakv", 1), ("merged", KT), ("xa_pre", KT), ("mem", KT), ("ffn_pre", KT),
          ("ffa", FK)]
SPB, NSP = offsets(SPLITS)
SPLIT_INS = [("mix_pre", KT), ("mlaq", 2), ("mlakv", 1), ("xa_pre", KT), ("mem", KT), ("ffn_pre", KT)]
SIB, NSI = offsets(SPLIT_INS)
assert NU % 2 == 0 and NCH % 2 == 0 and NTN % 2 == 0 and NHD % 2 == 0, (NU, NCH, NTN, NHD)

GAINS = [("mix_pre", KT), ("mix_post", KT), ("xa_pre", KT), ("mem", KT), ("xa_post", KT), ("ffn_pre", KT),
         ("ffn_post", KT), ("mlaq", QR // P), ("mlakv", KVR // P)]
GB, NG = offsets(GAINS)
PARTS = [("cmp", 2), ("br0", 4), ("br1", 4), ("qup", 6), ("kvup", 6), ("br2", 4), ("br3", 4), ("xo", 6)]
PTB, NPT = offsets(PARTS)
NMG = (NB - 1) * KT
RESIDS = [("mix_post", KT), ("xa_post", KT), ("ffn_post", KT)]
RB, NRS = offsets(RESIDS)
PJ_Q = 0
PJ_K = {"cmp": 4, "sel": 6, "win": 8, "swa": 4, "fox": 4, "xa": 2}
PJ_V = {"cmp": 5, "sel": 7, "win": 9, "swa": 5, "fox": 8, "xa": 4}
PJ_CQ, PJ_KV, PJ_N = 8, 8, 16

TWO_PI = 2 * math.pi
MAGIC = 1.5 * 2.0 ** 23


def two_pi_parts():
    parts, rest = [], TWO_PI
    for _ in range(3):
        unit = 2.0 ** (math.floor(math.log2(rest)) - 6)
        parts.append(math.floor(rest / unit) * unit)
        rest -= parts[-1]
    return parts + [rest]


class Pass:

    def __init__(self, name, grouped=False, slopes=False, sink=False, gate=None, filler=None, heads=H):
        self.name, self.grouped, self.slopes, self.sink = name, grouped, slopes, sink
        self.gate, self.filler, self.heads = gate, filler, heads
        self.steps = NT * heads

    def keys(self, i):
        if self.name == "cmp":
            return 0, NCP
        if self.name == "xa":
            return 0, M
        lo = max(i - 1, 0) if self.name == "swa" else 0
        return lo * P, (i + 1 - lo) * P

    def tiles(self, i):
        k0, w = self.keys(i)
        return (1, w) if w < P else (w // P, P)

    def slope(self, h):
        return 2.0 ** -(h + 1) if self.slopes else 1.0

    def item(self, h):
        if self.name == "mla":
            return h, h % 2, slice(0, HD + ROT)
        return h // 2, (h // 2) % 2, slice(h % 2 * HD, (h % 2 + 1) * HD)

    def key_slot(self, h):
        return h // (H // KVH) if self.grouped else self.item(h)[1]

    def staged_at(self, n):
        span = self.steps // dict(ITEMS)[self.name]
        return 0 if n == 0 else 1 if n == 1 else span * (n - 1) + 2


CMP = Pass("cmp", grouped=True, slopes=True, gate=0, filler=0)
SEL = Pass("sel", grouped=True, slopes=True, gate=1)
WIN = Pass("win", grouped=True, slopes=True, gate=2)
SWA = Pass("swa", grouped=True, slopes=True, sink=True, filler=1)
MLA = Pass("mla", filler=2)
FOX = Pass("fox", filler=3)
XA = Pass("xa", heads=XH)


def build(nc, x, mem, positions, mix_norm_pre, w_in, nsa_cmp_w, nsa_cmp_pe, swa_sinks, mla_q_norm, mla_w_q_up,
          mla_kv_norm, mla_w_kv_up, fox_f_bias, w_branch, w_gate, w_out, mix_norm_post, xa_norm_pre, xa_mem_norm,
          xa_w_q, xa_w_kv, xa_w_o, xa_norm_post, ffn_norm_pre, ffn_w_in, ffn_w_out, ffn_norm_post, out):
    ctx = ExitStack()
    with ctx:
        def sb(name, shape, dt=F32, stack=ctx):
            return stack.enter_context(nc.sbuf_tensor(name, shape, dt))

        def sem(name):
            return ctx.enter_context(nc.semaphore(name))

        trunk = sb("trunk", [P, KT, S])
        w_f32 = sb("w_f32", [P, 2, 1024])
        w_hi = sb("w_hi", [P, 2, 1024], F32R)
        w_lo = sb("w_lo", [P, 2, 1024], F32R)
        h_hi = sb("h_hi", [P, KT, S], F32R)
        h_lo = sb("h_lo", [P, KT, S], F32R)
        wide = sb("wide", [P, KT, S])
        squares = sb("squares", [P, 2, S])
        work = sb("work", [P, 2, S])
        ident = sb("ident", [P, P])
        ones = sb("ones", [P, P])
        dist = sb("dist", [P, (NT * (NT + 1) // 2) * P])
        dist_swa = sb("dist_swa", [P, NT, 2 * P])
        dist_cmp = sb("dist_cmp", [P, NT, NCP])
        mask = sb("mask", [P, S])
        cos = sb("cos", [R_END, S])
        sin = sb("sin", [R_END, S])
        narrow = sb("narrow", [R_END, S])
        gains = sb("gains", [P, L * NG])
        cmp_pe = sb("cmp_pe", [P, L * 2 * CMP_LEN])
        f_bias = sb("f_bias", [H, L])
        head_sink = sb("head_sink", [P, L * H, 2])
        head_now = sb("head_now", [P, H, 2])
        evac_scale = sb("evac_scale", [P, 2, 12])
        pick = sb("pick", [P, H], F32R)
        with ExitStack() as norms:
            square_sum = sb("square_sum", [P, S], F32, norms)
        cum_rows = sb("cum_rows", [P, S], F32R)
        row_sees = sb("row_sees", [P, NT])
        gate_tanh = sb("gate_tanh", [P, NT, 3 * H])
        coef = sb("coef", [P, 3, NT, H])
        mean_sq = sb("mean_sq", [P, NT])
        rstd = sb("rstd", [P, NT])
        half_neg = sb("half_neg", [P, NT])
        zero = sb("zero", [P, 1])
        neg_max = sb("neg_max", [P, 4])
        row_sum = sb("row_sum", [P, 4])
        sink_exp = sb("sink_exp", [P, 4])
        whole_sum = sb("whole_sum", [P, 4])
        over_sum = sb("over_sum", [P, 4])
        kg32 = sb("kg32", [HD, KVH, NCP])

        x_spill = nc.dram_tensor("x_spill", (P, KT, S), F32, kind="Internal").ap()
        mem_hat = nc.dram_tensor("mem_hat", (P, KT, M), F32, kind="Internal").ap()

        acc = [ctx.enter_context(nc.psum_tensor(f"acc{k}", [P, S], F32)) for k in range(2)]
        scores = [ctx.enter_context(nc.psum_tensor(f"scores{k}", [P, S], F32)) for k in range(2)]
        turn = [ctx.enter_context(nc.psum_tensor(f"turn{k}", [P, S], F32)) for k in range(2)]
        o_acc = [ctx.enter_context(nc.psum_tensor(f"o_acc{k}", [P, S], F32)) for k in range(2)]

        with ExitStack() as st:
            mem_in = sb("mem_in", [P, MT, D], stack=st)
            mem_t = sb("mem_t", [P, KT, M], stack=st)
            gain_rows = sb("gain_rows", [L * NG, P], stack=st)
            pe_rows = sb("pe_rows", [L * 2 * CMP_LEN, P], stack=st)
            pos_int = sb("pos_int", [P, S + NT], I32, stack=st)
            pos_row = sb("pos_row", [P, S + NT], stack=st)
            inv_row = sb("inv_row", [1, R_END], stack=st)
            ang = sb("ang", [R_END, 3, S], stack=st)
            mem_ms = sb("mem_ms", [P, 3, MT], stack=st)
        with ExitStack() as st:
            p_hi = sb("p_hi", [P, 2, S], F32R, st)
            p_lo = sb("p_lo", [P, 2, S], F32R, st)
            v_hi = sb("v_hi", [P, NT, BW], F32R, st)
            v_lo = sb("v_lo", [P, NT, BW], F32R, st)
            q_hi = sb("q_hi", [P, 2, S], F32R, st)
            q_lo = sb("q_lo", [P, 2, S], F32R, st)
            k_hi = sb("k_hi", [P, 2, S], F32R, st)
            k_lo = sb("k_lo", [P, 2, S], F32R, st)
            y_hi = sb("y_hi", [P, BW // P, S], F32R, st)
            y_lo = sb("y_lo", [P, BW // P, S], F32R, st)
            with ExitStack() as mix:
                proj = sb("proj", [P, PJ_N, S], F32, mix)
            with ExitStack() as cross:
                proj_x = sb("proj_x", [P, 6, S], F32, cross)
                m_hi = sb("m_hi", [P, KT, M], F32R, cross)
                m_lo = sb("m_lo", [P, KT, M], F32R, cross)
        with ExitStack() as st:
            a_hi = sb("a_hi", [P, FK, S], F32R, st)
            a_lo = sb("a_lo", [P, FK, S], F32R, st)

        wide_flat = wide[:, :, :].rearrange("p a b -> p (a b)")
        x_tok = wide_flat.rearrange("p (t d) -> p t d", t=NT)
        block_w = wide_flat.rearrange("p (l e) -> p l e", l=CMP_LEN)
        block_in = proj[:, 14:16, :].rearrange("p a b -> p (a b)").rearrange(
            "p (l c) -> p l c", l=CMP_LEN)
        m_f32 = wide_flat[:, 0:KT * M].rearrange("p (k m) -> p k m", k=KT)
        y_nsa = proj[:, 11:15, :]
        vc_feat = proj[:, 10, 0:NCP]
        logit, cum, exp_neg, softplus = (proj[0:H, 12 + n, :] for n in range(4))
        diag = squares[:, 0, :]
        SUMS, RBC = scores[0], scores[1]

        w_raw = [sem(f"w_raw{k}") for k in range(2)]
        misc_raw = sem("misc_raw")
        w_high = sem("w_high")
        w_ready = sem("w_ready")
        w_used = sem("w_used")
        part_ready = sem("part_ready")
        acc_free = [sem(f"acc_free{k}") for k in range(2)]
        q_high = sem("q_high")
        qk_ready = sem("qk_ready")
        kg_high = sem("kg_high")
        kg_low = sem("kg_low")
        scored = sem("scored")
        biased = sem("biased")
        exped = sem("exped")
        turned = sem("turned")
        turn_high = sem("turn_high")
        turn_ready = sem("turn_ready")
        applied = sem("applied")
        sink_added = sem("sink_added")
        inverted = sem("inverted")
        gated = sem("gated")
        divided = sem("divided")
        out_high = sem("out_high")
        nsa_out = sem("nsa_out")
        head_done = sem("head_done")
        squared = sem("squared")
        summed = sem("summed")
        ms_ready = sem("ms_ready")
        token_sums = sem("token_sums")
        rstd_ready = sem("rstd_ready")
        diag_ready = sem("diag_ready")
        rbc_ready = sem("rbc_ready")
        split_in = sem("split_in")
        split_high = sem("split_high")
        split_ready = sem("split_ready")
        scaled_out = sem("scaled_out")
        trunk_new = sem("trunk_new")
        merged = sem("merged")
        ng_turned = sem("ng_turned")
        ng_tanh = sem("ng_tanh")
        ng_coef = sem("ng_coef")
        blocks_zero = sem("blocks_zero")
        blocks_in = sem("blocks_in")
        blocks_tok = sem("blocks_tok")
        rope = sem("rope")
        rot_high = sem("rot_high")
        rot_ready = sem("rot_ready")
        forget = sem("forget")
        forget_act = sem("forget_act")
        x_saved = sem("x_saved")
        x_back = sem("x_back")
        mem_back = sem("mem_back")
        ff_tanh = sem("ff_tanh")
        s_scale = sem("s_scale")
        s_slot = sem("s_slot")
        s_const = sem("s_const")
        s_in = sem("s_in")
        s_rows = sem("s_rows")
        s_dve = sem("s_dve")
        s_pe = sem("s_pe")
        s_act = sem("s_act")
        s_angle = sem("s_angle")
        s_reduced = sem("s_reduced")
        s_far = sem("s_far")
        s_dist = sem("s_dist")
        s_masked = sem("s_masked")
        s_mem = sem("s_mem")
        s_mem_rstd = sem("s_mem_rstd")
        s_mem_turned = sem("s_mem_turned")
        s_mem_out = sem("s_mem_out")
        s_out = sem("s_out")

        def off(i):
            return i * (i + 1) // 2 * P

        def bias(ps, i):
            w = ps.keys(i)[1]
            if ps is CMP:
                return dist_cmp[:, i, :]
            if ps is SWA:
                return dist_swa[:, i, 0:w]
            if ps.slopes:
                return dist[:, off(i):off(i) + w]
            if ps is XA:
                return mask[:, 0:w]
            return mask[:, S - w:S]

        def raw_at(l, u, j):
            return l * (8 * NU) + j * 16 + 16 * (u // 2 + 1)

        def unit_at(l, u, j):
            return l * NU + 2 * j + u

        def free_at(l, c, q, j):
            return l * (NCH // 2) + q * j + (c // 2 + 1)

        def wait_apart(eng, signal, value):
            due = eng.to_reg(value)
            eng.wait_ge(s_const, 7)
            eng.wait_ge(signal, due)

        def wait_chunk_read(eng, l, name, c):
            c += CB[name]
            wait_apart(eng, acc_free[c % 2], free_at(l, c, 1, 0) + 1)

        def wait_chunk(eng, l, name, k, j, n):
            q = SHAPE[name.rstrip("0123")][0]
            if n == q - 1:
                eng.wait_ge(w_used, unit_at(l, UB[name] + k, j) + 3)
            else:
                eng.wait_ge(part_ready, l * NPT + (2 * (q - 1)) * j + (PTB[name] + k * (q - 1) + n + 1))

        def units(eng, name, body, first=0, count=None):
            n = (dict(UNITS)[name] if count is None else count)
            if n // 2 > 1:
                with eng.Fori(0, n // 2) as j:
                    body(first, j)
                    body(first + 1, j)
            elif n // 2 == 1:
                body(first, 0)
                body(first + 1, 0)
            if n % 2:
                body(first + n - 1, 0)

        SHAPE = {"misc": (1, KT, R_END), "nsa": (1, KT, P), "swa": (1, KT, P), "mla": (1, KT, P), "fox": (1, KT, P),
                 "gate": (1, KT, P), "br": (2, BW // P, P), "qup": (4, QR // P, HD + ROT), "kvup": (4, KVR // P, P),
                 "wout": (1, KT, P), "xq": (1, KT, P), "xkv": (1, KT, P), "xo": (4, XH * HD // P, P),
                 "ffin": (1, KT, P)}
        FF_UNITS = [8, 8, FK - 16]

        block = ctx.enter_context(nc.Block())

        @block.sync
        def _(sp):
            sp.dma_start(x_tok, x[0].rearrange("(t p) d -> p t d", p=P)).then_inc(s_in, 16)
            sp.dma_start(mem_in[:, :, :], mem[0].rearrange("(t p) d -> p t d", p=P)).then_inc(s_in, 16)

            w_in_v = w_in.rearrange("l (k p) n -> l p k n", p=P)
            gate_v = w_gate.rearrange("l b (k p) n -> l b p k n", p=P)
            branch_v = w_branch.rearrange("l b (k p) n -> l b p k n", p=P)
            q_up_v = mla_w_q_up.rearrange("l (k p) n -> l p k n", p=P)
            kv_up_v = mla_w_kv_up.rearrange("l (k p) n -> l p k n", p=P)
            out_v = w_out.rearrange("l (k p) n -> l p k n", p=P)
            xq_v = xa_w_q.rearrange("l (k p) n -> l p k n", p=P)
            xkv_v = xa_w_kv.rearrange("l (k p) n -> l p k n", p=P)
            xo_v = xa_w_o.rearrange("l (k p) n -> l p k n", p=P)
            ff_in_v = ffn_w_in.rearrange("l (k p) n -> l p k n", p=P)
            ff_out_v = ffn_w_out.rearrange("l (k p) n -> l p k n", p=P)

            def slot(u, kts, cols):
                return w_f32[:, u % 2, 0:kts * cols].rearrange("p (k n) -> p k n", k=kts)

            def load(l, name, k, j, src, kts, cols):
                u = UB[name] + k
                sp.wait_ge(w_ready, unit_at(l, u, j) + 1)
                sp.dma_start(slot(u, kts, cols), src).then_inc(w_raw[u % 2], 16)

            sp.wait_ge(s_slot, 1)
            with sp.Fori(0, L) as l:
                u = UB["misc"]
                sp.wait_ge(w_ready, unit_at(l, u, 0) + 1)
                s3 = slot(u, KT, P)
                sp.dma_start(s3[:, :, R_R:R_END], w_in_v[l, :, :, C_MKR:C_FQ]).then_inc(w_raw[u % 2], 16)
                with nc.allow_non_contiguous_dma(reason="narrow projections"):
                    sp.dma_start(s3[:, :, R_F:R_F + H], w_in_v[l, :, :, C_FF:IN_COLS]).then_inc(misc_raw, 16)
                    sp.dma_start(s3[:, :, R_G:R_G + 3 * H], w_in_v[l, :, :, C_NG:C_SQ]).then_inc(misc_raw, 16)

                def w_cols(view, name, c0):
                    def body(k, j):
                        load(l, name, k, j, view[:, :, bass.ds(c0 + k * P + j * (2 * P), P)], KT, P)
                    units(sp, name, body)

                def gate(b):
                    w_cols(gate_v[l, b], f"gate{b}", 0)

                def branch(b):
                    def body(k, j):
                        load(l, f"br{b}", k, j, branch_v[l, b, :, :, bass.ds(k * 256 + j * 512, 256)], BW // P, 256)
                    units(sp, f"br{b}", body)

                w_cols(w_in_v[l], "nsa", C_NQ)
                gate(0)
                branch(0)
                w_cols(w_in_v[l], "swa", C_SQ)
                gate(1)
                branch(1)
                w_cols(w_in_v[l], "mla", C_MQ)
                w = 4 * (HD + ROT)
                units(sp, "qup", lambda k, j: load(l, "qup", k, j, q_up_v[l, :, :, k * w:(k + 1) * w], QR // P, w))
                units(sp, "kvup", lambda k, j: load(l, "kvup", k, j, kv_up_v[l, :, :, k * 512:(k + 1) * 512], 1, 512))
                gate(2)
                branch(2)
                w_cols(w_in_v[l], "fox", C_FQ)
                gate(3)
                branch(3)
                w_cols(out_v[l], "wout", 0)
                w_cols(xq_v[l], "xq", 0)
                w_cols(xkv_v[l], "xkv", 0)
                units(sp, "xo", lambda k, j: load(l, "xo", k, j, xo_v[l, :, :, k * 512:(k + 1) * 512], 2, 512))
                units(sp, "ffin", lambda k, j: load(l, "ffin", k, j, ff_in_v[l, :, :, bass.ds(k * FF + j * P, P)],
                                                    KT, P))
                with sp.Fori(0, KT // 2) as c:
                    for half in range(2):
                        k0 = 0
                        for n, kts in enumerate(FF_UNITS):
                            load(l, "ffout", 3 * half + n, 3 * c,
                                 ff_out_v[l, :, k0:k0 + kts, bass.ds(c * (2 * P) + half * P, P)], kts, P)
                            k0 += kts
            for t in range(NT):
                sp.wait_ge(s_act, KT + 2 * (t + 1))
                sp.dma_start(out[0].rearrange("(t p) d -> p t d", p=P)[:, t, :], x_tok[:, t, :]).then_inc(s_out, 16)
            sp.wait_ge(s_out, 16 * NT)

        @block.gpsimd
        def _(pool):
            pool.sem_inc(summed, CREDIT)
            pool.memset(w_f32[:, 0, :], 0.0).then_inc(s_slot, 1)
            with nc.allow_non_contiguous_dma(reason="small inputs"):
                for name, vec in (("mix_pre", mix_norm_pre), ("mix_post", mix_norm_post), ("xa_pre", xa_norm_pre),
                                  ("mem", xa_mem_norm), ("xa_post", xa_norm_post), ("ffn_pre", ffn_norm_pre),
                                  ("ffn_post", ffn_norm_post), ("mlaq", mla_q_norm), ("mlakv", mla_kv_norm)):
                    n = vec.shape[1] // P
                    for l in range(L):
                        r = l * NG + GB[name]
                        pool.dma_start(gain_rows[r:r + n, :], vec[l].rearrange("(k p) -> k p", p=P)).then_inc(s_rows, 16)
                for h in range(KVH):
                    pool.dma_start(pe_rows[:, h * HD:(h + 1) * HD],
                                   nsa_cmp_pe.rearrange("l c n d -> (l c n) d")).then_inc(s_rows, 16)
                pool.dma_start(pos_int[:, 0:S], positions[0:1, :].to_broadcast([P, S])).then_inc(s_rows, 16)
                pool.dma_start(pos_int[:, S:S + NT], positions[0].rearrange("(t p) -> p t", p=P)).then_inc(s_rows, 16)
                pool.dma_start(f_bias[:, :], fox_f_bias.rearrange("l h -> h l")).then_inc(s_rows, 16)
                pool.dma_start(head_sink[:, :, 1],
                               swa_sinks.rearrange("(o l) h -> o (l h)", o=1).to_broadcast([P, L * H])).then_inc(s_rows, 16)
            pool.memset(ident[:, :], 0.0).then_inc(s_const, 1)
            pool.memset(mask[:, :], 0.0).then_inc(s_const, 1)
            pool.memset(row_sees[:, :], 1.0).then_inc(s_const, 1)
            pool.memset(inv_row[:, 0:R_R], 0.0)
            for n in range(ROT // 2):
                f = float(np.float32(10000.0 ** (-n / (ROT // 2))))
                pool.memset(inv_row[:, R_R + n:R_R + n + 1], -f)
                pool.memset(inv_row[:, R_R + ROT // 2 + n:R_R + ROT // 2 + n + 1], f)
            pool.memset(ones[:, :], 1.0)
            pool.memset(half_neg[:, :], -0.5)
            pool.memset(zero[:, :], 0.0)
            pool.memset(evac_scale[:, :, :], 1.0)
            pool.memset(pick[:, :].bitcast(F32), 0.0).then_inc(s_const, 1)
            pool.memset(dist_cmp[:, :, NC:NCP], BIG)
            pool.wait_ge(s_const, 4)
            pool.affine_select(out=ident[:, :], in_=ident[:, :], compare_op=ALU.not_equal, fill=1.0, base=0,
                               pattern=[[-1, P]], channel_multiplier=1).then_inc(s_const, 1)
            pool.memset(evac_scale[:, 1, 0:4], -(HD ** -0.5)).then_inc(s_scale, 1)
            pool.wait_ge(s_scale, 1)
            for c in range(4):
                pool.memset(evac_scale[0:HD, 0, c:c + 1], -(HD ** -0.5) / CMP.slope(2 * c))
                pool.memset(evac_scale[HD:P, 0, c:c + 1], -(HD ** -0.5) / CMP.slope(2 * c + 1)).then_inc(s_scale, 1)
            pool.wait_ge(s_scale, 5)
            pool.affine_select(out=mask[:, :], in_=mask[:, :], compare_op=ALU.is_ge, fill=BIG, base=S - P,
                               pattern=[[-1, S]], channel_multiplier=1).then_inc(s_const, 1)
            pool.affine_select(out=row_sees[:, :], in_=row_sees[:, :], compare_op=ALU.is_ge, fill=0.0,
                               base=-(CMP_LEN - 1), pattern=[[P, NT]], channel_multiplier=1).then_inc(s_const, 1)
            pool.wait_ge(s_dist, 2 * NT)
            for i in range(NT):
                w = (i + 1) * P
                d = dist[:, off(i):off(i) + w]
                pool.affine_select(out=d, in_=d, compare_op=ALU.is_ge, fill=BIG, base=i * P, pattern=[[-1, w]],
                                   channel_multiplier=1).then_inc(s_masked, 1)
                c = dist_cmp[:, i, 0:NC]
                pool.affine_select(out=c, in_=c, compare_op=ALU.is_ge, fill=BIG, base=i * P - (CMP_LEN - 1),
                                   pattern=[[-CMP_STRIDE, NC]], channel_multiplier=1).then_inc(s_masked, 1)
            pool.wait_ge(s_masked, 2 * NT)
            for i in range(NT):
                k0, w = SWA.keys(i)
                pool.affine_select(out=dist_swa[:, i, 0:w], in_=dist[:, off(i) + k0:off(i) + k0 + w],
                                   compare_op=ALU.is_gt, fill=BIG, base=WINDOW - i * P + k0, pattern=[[1, w]],
                                   channel_multiplier=-1).then_inc(s_masked, 1)
            pool.wait_ge(s_mem, 3)
            pool.tensor_tensor(mem_ms[:, 2, :], mem_ms[:, 1, :], half_neg[:, 0:MT], ALU.pow).then_inc(s_mem_rstd, 1)
            pool.wait_ge(s_mem, 3 + MT + KT)
            pool.dma_start(mem_hat, mem_t[:, :, :]).then_inc(s_mem_out, 16)
            pool.wait_ge(s_mem_out, 16)

            def power(l, name):
                for c in range(dict(NORMS)[name]):
                    sq = l * NSQ + (SQB[name] + c)
                    pool.wait_ge(squared, sq + 1)
                    if c == 0:
                        nc.gpsimd.tensor_tensor(square_sum[:, :], squares[:, 0, :], zero[:, 0:1].to_broadcast([P, S]),
                                                ALU.add).then_inc(summed, 1)
                    else:
                        pool.wait_ge(summed, sq + 2)
                        nc.gpsimd.tensor_tensor(square_sum[:, :], square_sum[:, :], squares[:, c % 2, :],
                                                ALU.add).then_inc(summed, 1)
                n = l * NNORM + NB_OF[name]
                wait_apart(pool, ms_ready, n + 1)
                pool.tensor_tensor(rstd[:, :], mean_sq[:, :], half_neg[:, :], ALU.pow).then_inc(rstd_ready, 1)

            with pool.Fori(0, L) as l:
                pool.wait_ge(s_act, KT)
                wait_apart(pool, trunk_new, l * NRS + 1)
                pool.dma_start(x_spill, trunk[:, :, :]).then_inc(x_saved, 16)
                for kv in range(KVH):
                    a, b = kv * HD, (kv + 1) * HD
                    c, d = (1 - kv) * HD, (2 - kv) * HD
                    pool.memset(block_w[a:b, :, c:d], 0.0).then_inc(blocks_zero, 1)
                wait_apart(pool, blocks_zero, l * 2 + 2)
                power(l, "mix_pre")
                for cv in range(2):
                    if cv == 1:
                        wait_chunk_read(pool, l, "cmp", 0)
                    for kv in range(KVH):
                        a, b = kv * HD, (kv + 1) * HD
                        pool.dma_start(block_w[a:b, :, a:b],
                                       nsa_cmp_w[l, cv].rearrange("n d e -> d n e")).then_inc(blocks_in, 16)
                power(l, "mlaq")
                power(l, "mlakv")
                wait_apart(pool, split_ready, l * NSP + SPB["merged"] + KT)
                pool.dma_start(trunk[:, :, :], x_spill).then_inc(x_back, 16)
                power(l, "mix_post")
                power(l, "xa_pre")
                wait_apart(pool, trunk_new, l * NRS + (RB["mix_post"] + KT + 1))
                pool.dma_start(m_f32, mem_hat).then_inc(mem_back, 16)
                for name in ("xa_post", "ffn_pre", "ffn_post"):
                    power(l, name)

        @block.scalar
        def _(act):
            def split_high_part(l, u, j):
                act.wait_ge(w_raw[u % 2], raw_at(l, u, j))
                act.wait_ge(w_used, unit_at(l, u, j) + 1)
                nc.scalar.activation(w_hi[:, u % 2, :], w_f32[:, u % 2, :], ACT.Copy).then_inc(w_high, 1)

            def next_unit(l, name, k, j):
                split_high_part(l, UB[name] + k + 1, j)

            def evac(l, name, k, j, n, out_ap, in_ap=None, func=ACT.Copy, scale=1.0):
                q = SHAPE[name.rstrip("0123")][0]
                c = CB[name] + k * q + n
                wait_chunk(act, l, name, k, j, n)
                src = acc[c % 2][0:out_ap.shape[0], 0:out_ap.shape[-1]]
                nc.scalar.activation(out_ap, src, func, scale=scale).then_inc(acc_free[c % 2], 1)

            def project(l, name, to, scale=1.0, table=None):
                q = SHAPE[name][0]

                def body(k, j):
                    next_unit(l, name, k, j)
                    for n in range(q):
                        by = scale if table is None else evac_scale[:, table, bass.ds(2 * j + k, 1)]
                        evac(l, name, k, j, n, to(k * q + n, 2 * q * j), scale=by)
                units(act, name, body)

            def square_chunk(l, name, c, src, scale=1.0):
                sq = l * NSQ + SQB[name] + c
                act.wait_ge(summed, sq + (2 if c == 0 else 1))
                if c == 0:
                    act.wait_ge(rbc_ready, l * NNORM + (NB_OF[name] + 1))
                nc.scalar.activation(squares[:, c % 2, :], src, ACT.Square, scale=scale).then_inc(squared, 1)

            def split_chunk(l, name, c, dst, src):
                act.wait_ge(split_in, l * NSI + (SIB[name] + c + 1))
                nc.scalar.activation(dst, src, ACT.Copy).then_inc(split_high, 1)

            def norm_split(l, name, before):
                act.wait_ge(w_used, unit_at(l, UB[before], 0) + 2)
                for c in range(KT):
                    split_chunk(l, name, c, h_hi[:, c, :], work[:, c % 2, :])

            def turn_high_part(l, name, n, k, dst, src):
                t = l * NTN + n + (TB[name] + k)
                act.wait_ge(turned, t + 3)
                nc.scalar.activation(dst, src, ACT.Copy).then_inc(turn_high, 1)

            def value_turns(l, name, count, rows, tiles):
                for n in range(count):
                    bank = turn[(TB[name] + n) % 2]
                    turn_high_part(l, name, 0, n, v_hi[0:rows, 0:tiles, n * P:(n + 1) * P],
                                   bank[0:rows, 0:tiles * P].rearrange("p (t f) -> p t f", t=tiles))

            def attend(l, ps, key_chunk=None):
                st = l * (4 * NHD) + 4 * HB[ps.name]
                items = dict(ITEMS)[ps.name]
                span = ps.steps // items
                buf = proj_x if ps is XA else proj
                keys = {"cmp": NCP, "xa": M}.get(ps.name, S)
                gate = f"gate{ps.filler}"

                def split_group_keys():
                    if ps is CMP:
                        wait_chunk_read(act, l, "cmp", 0)
                    act.wait_ge(scored, st + 4 * NT)
                    for kv in range(KVH):
                        for half in range(2):
                            src = kg32[:, kv, :] if ps is CMP else proj[kv * HD:(kv + 1) * HD, key_chunk, :]
                            ins = nc.scalar.activation(k_hi[half * HD:(half + 1) * HD, kv, 0:keys], src, ACT.Copy)
                    ins.then_inc(kg_high, 1)

                def stage(n):
                    act.wait_ge(scored, st + (4 * NT + span * (n - 1)))
                    if ps is MLA:
                        nc.scalar.activation(k_hi[0:HD, n % 2, :], proj[0:HD, PJ_KV + n, :], ACT.Copy)
                        nc.scalar.activation(q_hi[0:HD + ROT, n % 2, :], proj[0:HD + ROT, n, :], ACT.Copy).then_inc(q_high, 1)
                    else:
                        if not ps.grouped:
                            nc.scalar.activation(k_hi[:, n % 2, 0:keys], buf[:, PJ_K[ps.name] + n, 0:keys], ACT.Copy)
                        nc.scalar.activation(q_hi[:, n % 2, :], buf[:, n, :], ACT.Copy).then_inc(q_high, 1)

                def probabilities(s):
                    h, i = divmod(s, NT)
                    w = ps.keys(i)[1]
                    act.wait_ge(biased, st + (s + 3))
                    if ps.sink:
                        nc.scalar.activation(sink_exp[:, s % 4:s % 4 + 1], neg_max[:, s % 4:s % 4 + 1], ACT.Exp,
                                             bias=head_now[:, h, 1:2])
                    nc.scalar.activation(work[:, s % 2, 0:w], work[:, s % 2, 0:w], ACT.Exp,
                                         bias=neg_max[:, s % 4:s % 4 + 1], scale=-1.0,
                                         accum_out=row_sum[:, s % 4:s % 4 + 1]).then_inc(exped, 1)

                def high(s):
                    n, rows = ps.tiles(s % NT)
                    act.wait_ge(applied, st + (s + 1))
                    turn_high_part(l, ps.name, 0, s, p_hi[0:rows, s % 2, 0:n * P],
                                   turn[(TB[ps.name] + s) % 2][0:rows, 0:n * P])

                def out_high_part(h):
                    if ps is WIN:
                        if h % 2:
                            act.wait_ge(head_done, l * NHD + (HB[ps.name] + h + 3))
                            nc.scalar.activation(y_hi[:, h // 2, :], y_nsa[:, h // 2, :], ACT.Copy).then_inc(out_high, 1)
                    elif ps.gate is None:
                        act.wait_ge(applied, st + (4 * h + 6))
                        nc.scalar.activation(y_hi[h % 2 * HD:(h % 2 + 1) * HD, h // 2, :], o_acc[h % 2][0:HD, :],
                                             ACT.Copy).then_inc(out_high, 1)

                if ps.grouped:
                    split_group_keys()
                for s in range(ps.steps + 4):
                    for n in range(items):
                        if ps.staged_at(n) == s:
                            stage(n)
                    if s < ps.steps:
                        probabilities(s)
                    if 1 <= s <= ps.steps:
                        high(s - 1)
                    if ps.filler is not None and s % 4 == 0 and s <= ps.steps:
                        if s > 0:
                            k = s // 4 - 1
                            evac(l, gate, k, 0, 0, wide[:, k, :], func=ACT.Tanh, scale=0.5)
                        if s < ps.steps:
                            next_unit(l, gate, s // 4, 0)
                    if s >= 6 and (s - 6) % 4 == 0:
                        out_high_part((s - 6) // 4)
            def branch(l, b):
                units(act, f"br{b}", lambda k, j: next_unit(l, f"br{b}", k, j))

            def out_chunk(l, name, k, j, n, scale, nm, c):
                ch = CB[name] + c
                wait_chunk(act, l, name, k, j, n)
                square_chunk(l, nm, c, acc[ch % 2][:, :], scale)
                nc.scalar.activation(wide[:, c, :], acc[ch % 2][:, :], ACT.Copy, scale=scale).then_inc(acc_free[ch % 2], 1)

            for c in range(KT):
                act.wait_ge(s_pe, c + 2)
                nc.scalar.activation(trunk[:, c, :], turn[(c + 1) % 2][:, :], ACT.Copy).then_inc(s_act, 1)
            act.wait_ge(s_reduced, 1)
            r = slice(R_R, R_END)
            nc.scalar.activation(sin[r, :], ang[r, 0, :], ACT.Sin)
            nc.scalar.activation(cos[r, :], ang[r, 1, :], ACT.Sin)

            with act.Fori(0, L) as l:
                act.wait_ge(misc_raw, l * 32 + 32)
                split_high_part(l, 0, 0)
                for c in range(KT):
                    act.wait_ge(trunk_new, l * NRS + 1)
                    act.wait_ge(s_act, KT)
                    square_chunk(l, "mix_pre", c, trunk[:, c, :])
                norm_split(l, "mix_pre", "misc")
                next_unit(l, "misc", 0, 0)
                evac(l, "misc", 0, 0, 0, narrow[:, :])
                project(l, "nsa", lambda c, r_: proj[:, bass.ds(r_ + c, 1), :], table=0)
                act.wait_ge(ng_turned, l + 1)
                act.wait_ge(s_act, KT)
                nc.scalar.activation(gate_tanh[:, :, :], SUMS[:, 0:NT * 3 * H].rearrange("p (t g) -> p t g", t=NT),
                                     ACT.Tanh, scale=0.5).then_inc(ng_tanh, 1)
                value_turns(l, "v_cmp", 1, NCP, 1)
                attend(l, CMP)
                value_turns(l, "v_sel", 1, P, NT)
                attend(l, SEL, PJ_K["sel"])
                value_turns(l, "v_win", 1, P, NT)
                attend(l, WIN, PJ_K["win"])
                branch(l, 0)
                project(l, "swa", lambda c, r_: proj[:, bass.ds(r_ + c, 1), :], table=0)
                value_turns(l, "v_swa", 1, P, NT)
                attend(l, SWA, PJ_K["swa"])
                branch(l, 1)
                project(l, "mla", lambda c, r_: proj[:, bass.ds(r_ + (PJ_CQ + c), 1), :])
                wait_chunk_read(act, l, "mla", 1)
                wait_chunk_read(act, l, "mla", 2)
                for c in range(2):
                    square_chunk(l, "mlaq", c, proj[:, PJ_CQ + c, :])
                for c in range(2):
                    split_chunk(l, "mlaq", c, y_hi[:, c, :], work[:, c % 2, :])
                square_chunk(l, "mlakv", 0, proj[:, PJ_CQ + 2, :])
                split_chunk(l, "mlakv", 0, y_hi[:, 2, :], work[:, 0, :])
                project(l, "qup", lambda c, r_: proj[0:HD + ROT, c, :], scale=-(HD + ROT) ** -0.5)
                project(l, "kvup", lambda c, r_: proj[:, PJ_KV + c, :])
                act.wait_ge(rope, l * 36 + 37)
                for e in range(2):
                    nc.scalar.activation(k_hi[HD:HD + ROT, e, :], narrow[R_R:R_END, :], ACT.Copy).then_inc(rot_high, 1)
                value_turns(l, "v_mla", 4, P, NT)
                attend(l, MLA)
                branch(l, 2)
                project(l, "fox", lambda c, r_: proj[:, bass.ds(r_ + c, 1), :], table=1)
                act.wait_ge(forget, l * 9 + 2)
                nc.scalar.activation(exp_neg, logit, ACT.Exp, scale=-1.0).then_inc(forget_act, 1)
                act.wait_ge(forget_act, l * 2 + 1)
                nc.scalar.activation(softplus, exp_neg, ACT.Ln, bias=1.0).then_inc(forget_act, 1)
                value_turns(l, "v_fox", 4, P, NT)
                attend(l, FOX)
                branch(l, 3)
                act.wait_ge(w_used, unit_at(l, UB["wout"], 0) + 2)
                for c in range(KT):
                    act.wait_ge(merged, l * NMG + (NMG - KT + c + 1))
                    nc.scalar.activation(h_hi[:, c, :], trunk[:, c, :], ACT.Copy).then_inc(split_high, 1)
                for c in range(KT):
                    next_unit(l, "wout", c, 0)
                    out_chunk(l, "wout", c, 0, 0, 0.5, "mix_post", c)
                for c in range(KT):
                    act.wait_ge(trunk_new, l * NRS + (RB["mix_post"] + c + 2))
                    square_chunk(l, "xa_pre", c, trunk[:, c, :])
                norm_split(l, "xa_pre", "xq")
                for c in range(KT):
                    split_chunk(l, "mem", c, m_hi[:, c, :], work[:, c % 2, 0:M])
                project(l, "xq", lambda c, r_: proj_x[:, c, :], scale=-(HD ** -0.5))
                project(l, "xkv", lambda c, r_: proj_x[:, bass.ds(r_ + (2 + c), 1), 0:M])
                value_turns(l, "v_xa", 2, P, MT)
                attend(l, XA)
                for c in range(KT):
                    if c % 4 == 0:
                        next_unit(l, "xo", c // 4, 0)
                    out_chunk(l, "xo", c // 4, 0, c % 4, 1.0, "xa_post", c)
                for c in range(KT):
                    act.wait_ge(trunk_new, l * NRS + (RB["xa_post"] + c + 2))
                    square_chunk(l, "ffn_pre", c, trunk[:, c, :])
                norm_split(l, "ffn_pre", "ffin")

                def ff(j, last=False):
                    next_unit(l, "ffin", 0, j)
                    c = CB["ffin"]
                    wait_chunk(act, l, "ffin", 0, j, 0)
                    act.wait_ge(split_ready, l * NSP + j + SPB["ffa"])
                    nc.scalar.activation(work[:, 0, :], acc[c % 2][:, :], ACT.Tanh, scale=0.5).then_inc(ff_tanh, 1)
                    next_unit(l, "ffin", 1, j)
                    act.wait_ge(acc_free[(c + 1) % 2], free_at(l, c + 1, 1, j) + 1)
                    nc.scalar.activation(a_hi[:, bass.ds(j, 1), :], work[:, 0, :], ACT.Copy).then_inc(split_high, 1)
                with act.Fori(0, FK) as j:
                    ff(j)
                for c in range(KT):
                    for n in range(3):
                        if c < KT - 1 or n < 2:
                            next_unit(l, "ffout", 3 * c + n, 0)
                    ch = CB["ffout"] + c
                    act.wait_ge(w_used, unit_at(l, UB["ffout"] + 3 * c + 2, 0) + 3)
                    square_chunk(l, "ffn_post", c, acc[ch % 2][:, :])
                    nc.scalar.activation(wide[:, c, :], acc[ch % 2][:, :], ACT.Copy).then_inc(acc_free[ch % 2], 1)

            for n in range(2 * NT):
                act.wait_ge(s_pe, KT + 1 + n + 1)
                nc.scalar.activation(x_tok[:, n // 2, (n % 2) * S:(n % 2 + 1) * S], turn[n % 2][:, :],
                                     ACT.Copy).then_inc(s_act, 1)

        @block.tensor
        def _(pe):
            pe.sem_inc(w_used, CREDIT)
            pe.sem_inc(scored, 4 * NT)
            pe.sem_inc(turned, CREDIT)
            pe.sem_inc(applied, CREDIT)
            pe.sem_inc(rbc_ready, 1)

            def product(dst, lhs, rhs, n, count, last_sem=None, added=0):
                (lh, ll), (rh, rl) = lhs, rhs
                a, b = ((lh, rh), (lh, rl), (ll, rh))[n % 3]
                ins = nc.tensor.matmul(dst, a, b, start=(n == 0 and not added), stop=(n == count - 1))
                if last_sem is not None and n == count - 1:
                    ins.then_inc(last_sem, 1)
                return ins

            def weights(u, kts, cols, kt, c0, width):
                a = kt * cols + c0
                return w_hi[:, u % 2, a:a + width], w_lo[:, u % 2, a:a + width]

            def unit_terms(l, name, k, j, n0, n1, rhs, free=S):
                q, kts, width = SHAPE[name.rstrip("0123")]
                u = UB[name] + k
                per = 3 * kts
                for n in range(n0, n1):
                    m, r = divmod(n, per)
                    c = CB[name] + k * q + m
                    if n == 0:
                        pe.wait_ge(w_ready, unit_at(l, u, j) + 3)
                    if r == 0:
                        pe.wait_ge(acc_free[c % 2], free_at(l, c, q, j))
                    cols = P if name == "misc" else q * width
                    product(acc[c % 2][0:width, 0:free], weights(u, kts, cols, r // 3, m * width, width), rhs(r // 3),
                            r, per, w_used if m == q - 1 else part_ready)

            def whole_unit(l, name, k, j, rhs, free=S):
                q, kts, _ = SHAPE[name.rstrip("0123")]
                unit_terms(l, name, k, j, 0, 3 * q * kts, rhs, free)

            def h_rhs(kt):
                return h_hi[:, kt, :], h_lo[:, kt, :]

            def y_rhs(kt):
                return y_hi[:, kt, :], y_lo[:, kt, :]

            def spread_rstd(l, name):
                n = dict(NORMS)[name]
                pe.wait_ge(summed, l * NSQ + (SQB[name] + n + 2))
                for i in range(NT):
                    ins = nc.tensor.matmul(SUMS[:, i:i + 1], square_sum[:, i * P:(i + 1) * P], ones[:, 0:1],
                                           start=True, stop=True)
                ins.then_inc(token_sums, 1)
                pe.wait_ge(diag_ready, l * NNORM + NB_OF[name] + 1)
                nc.tensor.matmul(RBC[:, :], ones[:, :], diag, start=True, stop=True).then_inc(rbc_ready, 1)

            def turn_bank(l, name, n, k):
                t = TB[name] + k
                if name in ("v_cmp", "v_mla"):
                    wait_apart(pe, turn_ready, l * NTN + n + (t + 1))
                else:
                    pe.wait_ge(turn_ready, l * NTN + n + (t + 1))
                return turn[t % 2]

            def value_turns(l, name, count, src, rows=P, tiles=NT):
                for n in range(count):
                    bank = turn_bank(l, name, 0, n)
                    for t in range(tiles):
                        ins = nc.tensor.transpose(bank[0:rows, t * P:(t + 1) * P], src(n, t), ident[:, :])
                    ins.then_inc(turned, 1)

            def attend(l, ps):
                st = l * (4 * NHD) + 4 * HB[ps.name]
                gate = f"gate{ps.filler}"

                def gate_terms(n0, n1):
                    for k in range(KT):
                        a, b = max(n0 - 24 * k, 0), min(n1 - 24 * k, 24)
                        if ps.filler is not None and a < b:
                            unit_terms(l, gate, k, 0, a, b, h_rhs)

                def score(s):
                    h, i = divmod(s, NT)
                    k0, w = ps.keys(i)
                    item, slot, rows = ps.item(h)
                    if i == 0:
                        pe.wait_ge(qk_ready, l * NIT + (IB[ps.name] + item + 1))
                    pe.wait_ge(biased, st + (s + 1))
                    q = [t[rows, slot, i * P:(i + 1) * P] for t in (q_hi, q_lo)]
                    k = [t[rows, ps.key_slot(h), k0:k0 + w] for t in (k_hi, k_lo)]
                    if ps is FOX:
                        c = slice(rows.start, rows.start + 32 + H)
                        nc.tensor.matmul(scores[s % 2][:, 0:w], pick[c, h:h + 1].to_broadcast([32 + H, P]),
                                         cum_rows[c, k0:k0 + w], start=True, stop=False)
                    first = 1 if ps is FOX else 0
                    for n in range(3):
                        product(scores[s % 2][:, 0:w], q, k, n, 3, scored, first)

                def turn_probs(s):
                    n, w = ps.tiles(s % NT)
                    bank = turn_bank(l, ps.name, 0, s)
                    pe.wait_ge(divided, st + (s + 1))
                    for t in range(n):
                        ins = nc.tensor.transpose(bank[0:w, t * P:(t + 1) * P], work[:, s % 2, t * w:(t + 1) * w],
                                                  ident[:, :])
                    ins.then_inc(turned, 1)

                def apply(s):
                    h, i = divmod(s, NT)
                    n, w = ps.tiles(i)
                    t0 = ps.keys(i)[0] // P
                    v0 = (h // (H // KVH) if ps.grouped else h) * HD
                    if i == 0:
                        pe.wait_ge(head_done, l * NHD + (HB[ps.name] + h + 1))
                    pe.wait_ge(turn_ready, l * NTN + (TB[ps.name] + s + 3))
                    for t in range(n):
                        vals = [x_[0:w, t0 + t, v0:v0 + HD] for x_ in (v_hi, v_lo)]
                        probs = [x_[0:w, s % 2, t * P:(t + 1) * P] for x_ in (p_hi, p_lo)]
                        for m in range(3):
                            product(o_acc[h % 2][0:HD, i * P:(i + 1) * P], vals, probs, 3 * t + m, 3 * n, applied)

                gate_terms(0, 12)
                score(0)
                for s in range(ps.steps + 2):
                    if s + 1 < ps.steps:
                        score(s + 1)
                    gate_terms(12 + 6 * s, 18 + 6 * s)
                    if 1 <= s <= ps.steps:
                        turn_probs(s - 1)
                    if s >= 2:
                        apply(s - 2)

            def branch(l, b):
                if b == 0:
                    wait_apart(pe, nsa_out, l * 4 + 4)
                else:
                    wait_apart(pe, head_done, l * NHD + (HB[("swa", "mla", "fox")[b - 1]] + H + 2))
                units(pe, f"br{b}", lambda k, j: whole_unit(l, f"br{b}", k, j, y_rhs))

            def when_split(l, name, rhs):
                waited = set()

                def of_chunk(kt):
                    if kt not in waited:
                        pe.wait_ge(split_ready, l * NSP + (SPB[name] + kt + 1))
                    waited.add(kt)
                    return rhs(kt)
                return of_chunk

            def project(l, name, rhs=h_rhs, free=S, after=None):
                count = dict(UNITS)[name]
                if after is None:
                    units(pe, name, lambda k, j: whole_unit(l, name, k, j, rhs, free))
                    return

                whole_unit(l, name, 0, 0, when_split(l, after, rhs), free)
                if count > 1:
                    whole_unit(l, name, 1, 0, rhs, free)
                if count > 2:
                    with pe.Fori(0, count // 2 - 1) as j:
                        whole_unit(l, name, 2, j, rhs, free)
                        whole_unit(l, name, 3, j, rhs, free)

            def wait_split(l, name, n):
                wait_apart(pe, split_ready, l * NSP + SPB[name] + n)

            pe.wait_ge(s_const, 7)
            pe.wait_ge(s_rows, 16 * (2 * len(GAINS) + KVH + 4))
            nc.tensor.transpose(turn[0][:, 0:L * NG], gain_rows[:, :], ident[0:L * NG, 0:L * NG])
            nc.tensor.transpose(turn[0][:, P:P + L * 2 * CMP_LEN], pe_rows[:, :], ident[:, :]).then_inc(s_pe, 1)
            pe.wait_ge(s_dve, 1)
            nc.tensor.matmul(scores[0][0:R_END, :], inv_row[:, :], pos_row[0:1, 0:S], start=True,
                             stop=True).then_inc(s_angle, 1)
            pe.wait_ge(s_in, 32)
            for c in range(KT):
                if c == 1:
                    pe.wait_ge(s_dve, 3)
                if c >= 2:
                    pe.wait_ge(s_act, c - 1)
                for t in range(NT):
                    ins = nc.tensor.transpose(turn[(c + 1) % 2][:, t * P:(t + 1) * P], x_tok[:, t, c * P:(c + 1) * P],
                                              ident[:, :])
                ins.then_inc(s_pe, 1)
            pe.wait_ge(s_mem, 3 + MT)
            for c in range(KT):
                if c >= 2:
                    pe.wait_ge(s_mem, 3 + MT + c - 1)
                for t in range(MT):
                    ins = nc.tensor.transpose(o_acc[c % 2][:, t * P:(t + 1) * P], mem_in[:, t, c * P:(c + 1) * P],
                                              ident[:, :])
                ins.then_inc(s_mem_turned, 1)
            pe.wait_ge(s_act, KT)
            pe.wait_ge(s_dve, 4)

            with pe.Fori(0, L) as l:
                spread_rstd(l, "mix_pre")
                project(l, "misc", after="mix_pre")
                project(l, "nsa")
                wait_chunk_read(pe, l, "misc", 0)
                g = slice(R_G, R_G + 3 * H)
                for t in range(NT):
                    ins = nc.tensor.transpose(SUMS[:, t * 3 * H:(t + 1) * 3 * H], narrow[g, t * P:(t + 1) * P],
                                              ident[g, g])
                ins.then_inc(ng_turned, 1)
                for cv in range(2):
                    c = CB["cmp"] + cv
                    pe.wait_ge(blocks_in, l * 64 + 32 * (cv + 1))
                    if cv == 0:
                        pe.wait_ge(blocks_zero, l * 2 + 2)
                    pe.wait_ge(blocks_tok, l * 6 + 3 * (cv + 1))
                    pe.wait_ge(acc_free[c % 2], free_at(l, c, 1, 0))
                    for n in range(CMP_LEN):
                        ins = nc.tensor.matmul(acc[c % 2][:, 0:NCP], block_w[:, n, :], block_in[:, n, :],
                                               start=(n == 0), stop=(n == CMP_LEN - 1))
                    ins.then_inc(part_ready, 1)
                wait_chunk_read(pe, l, "cmp", 1)
                bank = turn_bank(l, "v_cmp", 0, 0)
                nc.tensor.transpose(bank[0:NCP, 0:P], vc_feat, ident[:, :]).then_inc(turned, 1)
                wait_apart(pe, ng_tanh, l + 1)
                attend(l, CMP)
                value_turns(l, "v_sel", 1, lambda n, t: proj[:, PJ_V["sel"], t * P:(t + 1) * P])
                attend(l, SEL)
                value_turns(l, "v_win", 1, lambda n, t: proj[:, PJ_V["win"], t * P:(t + 1) * P])
                attend(l, WIN)
                branch(l, 0)
                project(l, "swa")
                wait_chunk_read(pe, l, "swa", 5)
                value_turns(l, "v_swa", 1, lambda n, t: proj[:, PJ_V["swa"], t * P:(t + 1) * P])
                attend(l, SWA)
                branch(l, 1)
                project(l, "mla")
                spread_rstd(l, "mlaq")
                spread_rstd(l, "mlakv")
                wait_split(l, "mlaq", 2)
                project(l, "qup", y_rhs)
                wait_split(l, "mlakv", 1)
                project(l, "kvup", lambda kt: (y_hi[:, 2, :], y_lo[:, 2, :]))
                wait_chunk_read(pe, l, "kvup", 7)
                for n in range(4):
                    bank = turn_bank(l, "v_mla", 0, n)
                    for t in range(NT):
                        for e in range(2):
                            ins = nc.tensor.transpose(bank[:, t * P + e * HD:t * P + (e + 1) * HD],
                                                      proj[HD:P, PJ_KV + 2 * n + e, t * P:(t + 1) * P],
                                                      ident[HD:P, HD:P])
                    ins.then_inc(turned, 1)
                attend(l, MLA)
                branch(l, 2)
                project(l, "fox")
                wait_chunk_read(pe, l, "fox", 11)
                value_turns(l, "v_fox", 4, lambda n, t: proj[:, PJ_V["fox"] + n, t * P:(t + 1) * P])
                attend(l, FOX)
                branch(l, 3)
                for c in range(KT):
                    if c == 0:
                        whole_unit(l, "wout", c, 0, when_split(l, "merged", h_rhs))
                    else:
                        whole_unit(l, "wout", c, 0, h_rhs)
                spread_rstd(l, "mix_post")
                spread_rstd(l, "xa_pre")
                project(l, "xq", after="xa_pre")
                wait_split(l, "mem", KT)
                project(l, "xkv", lambda kt: (m_hi[:, kt, :], m_lo[:, kt, :]), free=M)
                wait_chunk_read(pe, l, "xkv", 3)
                value_turns(l, "v_xa", 2, lambda n, t: proj_x[:, PJ_V["xa"] + n, t * P:(t + 1) * P], tiles=MT)
                attend(l, XA)
                pe.wait_ge(head_done, l * NHD + NHD + 2)
                for c in range(KT):
                    unit_terms(l, "xo", c // 4, 0, 6 * (c % 4), 6 * (c % 4) + 6, y_rhs)
                spread_rstd(l, "xa_post")
                spread_rstd(l, "ffn_pre")
                project(l, "ffin", after="ffn_pre")
                for c in range(KT):
                    ch = CB["ffout"] + c
                    n = kt0 = 0
                    pe.wait_ge(acc_free[ch % 2], free_at(l, ch, 1, 0))
                    for k, kts in enumerate(FF_UNITS):
                        u = UB["ffout"] + 3 * c + k
                        pe.wait_ge(w_ready, unit_at(l, u, 0) + 3)
                        for kt in range(kts):
                            if c == 0:
                                pe.wait_ge(split_ready, l * NSP + (SPB["ffa"] + kt0 + kt + 1))
                            for m in range(3):
                                ins = product(acc[ch % 2][:, :], weights(u, kts, P, kt, 0, P),
                                              (a_hi[:, kt0 + kt, :], a_lo[:, kt0 + kt, :]), n, 3 * FK)
                                n += 1
                        ins.then_inc(w_used, 1)
                        kt0 += kts
                spread_rstd(l, "ffn_post")

            pe.wait_ge(trunk_new, L * NRS + 1)
            for n in range(2 * NT):
                t, half = divmod(n, 2)
                if n >= 2:
                    pe.wait_ge(s_act, KT + n - 1)
                for c in range(NT):
                    ins = nc.tensor.transpose(turn[n % 2][:, c * P:(c + 1) * P],
                                              trunk[:, half * NT + c, t * P:(t + 1) * P], ident[:, :])
                ins.then_inc(s_pe, 1)

        @block.vector
        def _(dve):
            dve.sem_inc(w_ready, CREDIT)
            dve.sem_inc(trunk_new, 1)
            dve.sem_inc(rope, 1)
            dve.sem_inc(acc_free[0], 1)
            dve.sem_inc(acc_free[1], 1)
            dve.sem_inc(biased, CREDIT)
            dve.sem_inc(turn_ready, CREDIT)
            dve.sem_inc(head_done, CREDIT)

            def split_rest(l, u, j):
                dve.wait_ge(w_high, unit_at(l, u, j) + 1)
                nc.vector.tensor_tensor(w_lo[:, u % 2, :], w_f32[:, u % 2, :], w_hi[:, u % 2, :].bitcast(F32),
                                        ALU.subtract).then_inc(w_ready, 1)

            def next_unit(l, name, k, j):
                split_rest(l, UB[name] + k + 1, j)

            def gain(l, name, c):
                return gains[:, bass.ds(l * NG + (GB[name] + c), 1)]

            def rstd_rows(l, name, width):
                n = dict(NORMS)[name]
                dve.wait_ge(token_sums, l * NNORM + NB_OF[name] + 1)
                nc.vector.tensor_scalar(mean_sq[:, :], SUMS[:, 0:NT], 1.0 / width, EPS, ALU.mult,
                                        ALU.add).then_inc(ms_ready, 1)
                dve.wait_ge(rstd_ready, l * NNORM + NB_OF[name] + 1)
                nc.vector.tensor_tensor(diag.rearrange("p (t c) -> p t c", t=NT),
                                        ident[:, :].unsqueeze(1).to_broadcast([P, NT, P]),
                                        rstd[:, :].unsqueeze(2).to_broadcast([P, NT, P]), ALU.mult).then_inc(diag_ready, 1)
                dve.wait_ge(rbc_ready, l * NNORM + (NB_OF[name] + 2))

            def rest_of_chunk(l, name, c, dst, src, high):
                dve.wait_ge(split_high, l * NSP + (SPB[name] + c + 1))
                nc.vector.tensor_tensor(dst, src, high.bitcast(F32), ALU.subtract).then_inc(split_ready, 1)

            def norm(l, name, width, src, hi, lo):
                n = dict(NORMS)[name]
                rstd_rows(l, name, width)
                for c in range(n + 1):
                    if c < n:
                        if c > 1:
                            dve.wait_ge(split_ready, l * NSP + (SPB[name] + c - 1))
                        nc.vector.scalar_tensor_tensor(work[:, c % 2, :], src(c), gain(l, name, c), RBC[:, :], ALU.mult,
                                                       ALU.mult).then_inc(split_in, 1)
                    if c > 0:
                        rest_of_chunk(l, name, c - 1, lo(c - 1), work[:, (c - 1) % 2, :], hi(c - 1))

            def h_norm(l, name):
                norm(l, name, D, lambda c: trunk[:, c, :], lambda c: h_hi[:, c, :], lambda c: h_lo[:, c, :])

            def add_to_trunk(l, name, phase):
                rstd_rows(l, name, D)
                wait_chunk_read(dve, l, phase, KT - 1)
                for c in range(KT + 1):
                    at = l * NRS + (RB[name] + c)
                    if c < KT:
                        if c > 1:
                            dve.wait_ge(trunk_new, at)
                        nc.vector.scalar_tensor_tensor(work[:, c % 2, :], wide[:, c, :], gain(l, name, c), RBC[:, :],
                                                       ALU.mult, ALU.mult).then_inc(scaled_out, 1)
                    if c > 0:
                        dve.wait_ge(scaled_out, at)
                        nc.vector.tensor_tensor(trunk[:, c - 1, :], trunk[:, c - 1, :], work[:, (c - 1) % 2, :],
                                                ALU.add).then_inc(trunk_new, 1)

            def turn_rest(l, name, n, k, dst, bank, high):
                t = l * NTN + n + (TB[name] + k)
                dve.wait_ge(turn_high, t + 1)
                nc.vector.tensor_tensor(dst, bank, high.bitcast(F32), ALU.subtract).then_inc(turn_ready, 1)

            def value_turns(l, name, count, rows, tiles):
                for n in range(count):
                    bank = turn[(TB[name] + n) % 2][0:rows, 0:tiles * P].rearrange("p (t f) -> p t f", t=tiles)
                    at = (slice(0, rows), slice(0, tiles), slice(n * P, (n + 1) * P))
                    turn_rest(l, name, 0, n, v_lo[at], bank, v_hi[at])

            def attend(l, ps, key_chunk=None):
                st = l * (4 * NHD) + 4 * HB[ps.name]
                items = dict(ITEMS)[ps.name]
                buf = proj_x if ps is XA else proj
                keys = {"cmp": NCP, "xa": M}.get(ps.name, S)

                def split_group_keys():
                    dve.wait_ge(kg_high, l * NKG + (KGB[ps.name] + 1))
                    own = [slice(0, HD) if ps is CMP else slice(kv * HD, (kv + 1) * HD) for kv in range(KVH)]
                    for kv in range(KVH):
                        src = kg32[:, kv, :] if ps is CMP else proj[own[kv], key_chunk, :]
                        ins = nc.vector.tensor_tensor(k_lo[own[kv], kv, 0:keys], src,
                                                      k_hi[own[kv], kv, 0:keys].bitcast(F32), ALU.subtract)
                    ins.then_inc(kg_low, 1)
                    dve.wait_ge(kg_low, l * NKG + (KGB[ps.name] + 1))
                    for kv in range(KVH):
                        other = slice(HD, P) if own[kv].start == 0 else slice(0, HD)
                        nc.vector.tensor_copy(k_lo[other, kv, 0:keys], k_lo[own[kv], kv, 0:keys].bitcast(F32))

                def stage(n):
                    dve.wait_ge(q_high, l * NIT + (IB[ps.name] + n + 1))
                    if ps is MLA:
                        nc.vector.tensor_tensor(k_lo[0:HD, n % 2, :], proj[0:HD, PJ_KV + n, :],
                                                k_hi[0:HD, n % 2, :].bitcast(F32), ALU.subtract)
                    elif not ps.grouped:
                        nc.vector.tensor_tensor(k_lo[:, n % 2, 0:keys], buf[:, PJ_K[ps.name] + n, 0:keys],
                                                k_hi[:, n % 2, 0:keys].bitcast(F32), ALU.subtract)
                    rows = slice(0, HD + ROT if ps is MLA else P)
                    nc.vector.tensor_tensor(q_lo[rows, n % 2, :], buf[rows, n, :], q_hi[rows, n % 2, :].bitcast(F32),
                                            ALU.subtract).then_inc(qk_ready, 1)

                def bias_scores(s):
                    h, i = divmod(s, NT)
                    w = ps.keys(i)[1]
                    dve.wait_ge(turned, l * NTN + (TB[ps.name] + s + 1))
                    due = dve.to_reg(st + (4 * NT + s + 1))
                    dve.wait_ge(s_masked, 3 * NT)
                    dve.wait_ge(scored, due)
                    nc.vector.tensor_tensor_reduce(
                        work[:, s % 2, 0:w], scores[s % 2][:, 0:w], bias(ps, i), ps.slope(h),
                        head_now[:, h, 0:1] if ps.sink else NO_SINK, ALU.add, ALU.min,
                        neg_max[:, s % 4:s % 4 + 1]).then_inc(biased, 1)

                def divide(s):
                    h, i = divmod(s, NT)
                    c = slice(s % 4, s % 4 + 1)
                    dve.wait_ge(exped, st + (s + 1))
                    total = row_sum[:, c]
                    if ps.sink:
                        total = whole_sum[:, c]
                        nc.vector.tensor_tensor(total, row_sum[:, c], sink_exp[:, c], ALU.add).then_inc(sink_added, 1)
                        dve.wait_ge(sink_added, st + (s + 1))
                    nc.vector.reciprocal(over_sum[:, c], total).then_inc(inverted, 1)
                    by = over_sum[:, c]
                    if ps is CMP and s == 0:
                        dve.wait_ge(ng_coef, l * 2 + 2)
                    dve.wait_ge(inverted, st + (s + 1))
                    if ps.gate is not None:
                        by = whole_sum[:, c]
                        nc.vector.tensor_tensor(by, over_sum[:, c], coef[:, ps.gate, i, h:h + 1],
                                                ALU.mult).then_inc(gated, 1)
                        dve.wait_ge(gated, st + (s + 1))
                    w = ps.keys(i)[1]
                    nc.vector.tensor_scalar(work[:, s % 2, 0:w], work[:, s % 2, 0:w], by, None,
                                            ALU.mult).then_inc(divided, 1)

                def out(h):
                    rows = slice(h % 2 * HD, (h % 2 + 1) * HD)
                    src = o_acc[h % 2][0:HD, :]
                    if ps.gate is None:
                        dve.wait_ge(out_high, l * NOUT + (OB[ps.name] + h + 1))
                        nc.vector.tensor_tensor(y_lo[rows, h // 2, :], src, y_hi[rows, h // 2, :].bitcast(F32),
                                                ALU.subtract).then_inc(head_done, 1)
                        return
                    dst = y_nsa[rows, h // 2, :]
                    dve.wait_ge(applied, st + (4 * h + 6))
                    if ps is CMP:
                        nc.vector.tensor_copy(dst, src).then_inc(head_done, 1)
                    else:
                        nc.vector.tensor_tensor(dst, src, dst, ALU.add).then_inc(head_done, 1)

                def nsa_rest(c):
                    dve.wait_ge(out_high, l * NOUT + (OB["nsa"] + c + 1))
                    nc.vector.tensor_tensor(y_lo[:, c, :], y_nsa[:, c, :], y_hi[:, c, :].bitcast(F32),
                                            ALU.subtract).then_inc(nsa_out, 1)

                if ps.grouped:
                    split_group_keys()
                if ps.sink:
                    nc.vector.tensor_copy(head_now[:, :, :], head_sink[:, bass.ds(l * H, H), :])
                    dve.sem_inc(sink_added, 4 * HB[ps.name])
                for s in range(ps.steps + 4):
                    for n in range(items):
                        if ps.staged_at(n) == s:
                            stage(n)
                    if s < ps.steps:
                        bias_scores(s)
                    if 1 <= s <= ps.steps:
                        divide(s - 1)
                    if 2 <= s <= ps.steps + 1:
                        t = s - 2
                        n, rows = ps.tiles(t % NT)
                        turn_rest(l, ps.name, 0, t, p_lo[0:rows, t % 2, 0:n * P],
                                  turn[(TB[ps.name] + t) % 2][0:rows, 0:n * P], p_hi[0:rows, t % 2, 0:n * P])
                    if ps.filler is not None and s % 4 == 0 and s < ps.steps:
                        next_unit(l, f"gate{ps.filler}", s // 4, 0)
                    if s >= 6 and (s - 6) % 4 == 0:
                        out((s - 6) // 4)
                    if ps is WIN and s >= 11 and (s - 11) % 8 == 0:
                        nsa_rest((s - 11) // 8)

            def branch(l, b):
                def body(k, j):
                    next_unit(l, f"br{b}", k, j)
                    for n in range(2):
                        c = CB[f"br{b}"] + 2 * k + n
                        i = 4 * j + 2 * k + n
                        wait_chunk(dve, l, f"br{b}", k, j, n)
                        if b == 0:
                            dve.wait_ge(x_saved, l * 16 + 16)
                            dst = trunk[:, bass.ds(i, 1), :]
                        else:
                            dst = work[:, n, :]
                        nc.vector.scalar_tensor_tensor(dst, wide[:, bass.ds(i, 1), :], 1.0, acc[c % 2][:, :], ALU.add,
                                                       ALU.mult).then_inc(acc_free[c % 2], 1)
                        if b > 0:
                            dve.wait_ge(acc_free[c % 2], free_at(l, c, 2, j) + 1)
                            m = trunk[:, bass.ds(i, 1), :]
                            nc.vector.tensor_tensor(m, m, dst, ALU.add).then_inc(merged, 1)
                units(dve, f"br{b}", body)

            def project(l, name):
                units(dve, name, lambda k, j: next_unit(l, name, k, j))

            def rotate(l, n, rows_of):
                at = l * 36 + (4 * n + 1)
                r = slice(R_R, R_END)
                half = ROT // 2
                wait_apart(dve, rope, at)
                nc.vector.stream_shuffle(work[r, 0, :], rows_of, list(range(half, ROT)) + list(range(half))).then_inc(rope, 1)
                nc.vector.tensor_tensor(work[r, 1, :], rows_of, cos[r, :], ALU.mult).then_inc(rope, 1)
                dve.wait_ge(rope, at + 1)
                nc.vector.tensor_tensor(work[r, 0, :], work[r, 0, :], sin[r, :], ALU.mult).then_inc(rope, 1)
                dve.wait_ge(rope, at + 3)
                nc.vector.tensor_tensor(rows_of, work[r, 0, :], work[r, 1, :], ALU.add).then_inc(rope, 1)

            dve.wait_ge(s_rows, 16 * (2 * len(GAINS) + KVH + 4))
            nc.vector.tensor_copy(pos_row[:, :], pos_int[:, :]).then_inc(s_dve, 1)
            dve.wait_ge(s_pe, 1)
            nc.vector.tensor_copy(gains[:, :], turn[0][:, 0:L * NG]).then_inc(s_dve, 1)
            nc.vector.tensor_copy(cmp_pe[:, :], turn[0][:, P:P + L * 2 * CMP_LEN]).then_inc(s_dve, 1)
            dve.wait_ge(s_angle, 1)
            r = slice(R_R, R_END)
            nc.vector.tensor_copy(ang[r, 0, :], scores[0][r, :]).then_inc(s_dve, 1)
            dve.wait_ge(s_const, 7)
            nc.vector.tensor_scalar(head_sink[:, :, 0], head_sink[:, :, 1], -1.0, None, ALU.mult)
            for b in range(0, P, 32):
                nc.vector.tensor_copy(pick[b:b + H, :], ident[b:b + H, b:b + H])
            for i in range(NT):
                w = (i + 1) * P
                pc = pos_row[:, S + i:S + i + 1]
                far, far_cmp = dist[:, off(i):off(i) + w], dist_cmp[:, i, 0:NC]
                nc.vector.tensor_scalar(far, pos_row[:, 0:w], pc, None, ALU.subtract).then_inc(s_far, 1)
                nc.vector.tensor_scalar(far_cmp, pos_row[:, CMP_LEN - 1:S:CMP_STRIDE], pc, None,
                                        ALU.subtract).then_inc(s_far, 1)
                dve.wait_ge(s_far, 2 * i + 1)
                nc.vector.scalar_tensor_tensor(far, far, -1.0, far, ALU.mult, ALU.max).then_inc(s_dist, 1)
                dve.wait_ge(s_far, 2 * i + 2)
                nc.vector.scalar_tensor_tensor(far_cmp, far_cmp, -1.0, far_cmp, ALU.mult, ALU.max).then_inc(s_dist, 1)
            dve.wait_ge(s_in, 32)
            for t in range(MT):
                if t > 0:
                    dve.wait_ge(s_mem, t)
                nc.vector.tensor_tensor_reduce(squares[:, :, :].rearrange("p a b -> p (a b)"), mem_in[:, t, :],
                                               mem_in[:, t, :], 1.0, 0.0, ALU.mult, ALU.add,
                                               mem_ms[:, 0, t:t + 1]).then_inc(s_mem, 1)
            dve.wait_ge(s_mem, 2)
            nc.vector.tensor_scalar(mem_ms[:, 1, :], mem_ms[:, 0, :], 1.0 / D, EPS, ALU.mult, ALU.add).then_inc(s_mem, 1)
            dve.wait_ge(s_mem_rstd, 1)
            for t in range(MT):
                nc.vector.tensor_scalar(mem_in[:, t, :], mem_in[:, t, :], mem_ms[:, 2, t:t + 1], None,
                                        ALU.mult).then_inc(s_mem, 1)
            for c in range(KT):
                dve.wait_ge(s_mem_turned, c + 1)
                nc.vector.tensor_copy(mem_t[:, c, :], o_acc[c % 2][:, 0:M]).then_inc(s_mem, 1)
            a, t = ang[r, 0, :], ang[r, 1, :]
            n = 4
            for many in (4096.0, 1.0):
                dve.wait_ge(s_dve, n)
                nc.vector.tensor_scalar(t, a, 1.0 / (TWO_PI * many), MAGIC, ALU.mult, ALU.add).then_inc(s_dve, 1)
                dve.wait_ge(s_dve, n + 1)
                nc.vector.tensor_scalar(t, t, MAGIC, None, ALU.subtract).then_inc(s_dve, 1)
                n += 2
                for part in two_pi_parts():
                    dve.wait_ge(s_dve, n)
                    nc.vector.scalar_tensor_tensor(a, t, -part * many, a, ALU.mult, ALU.add).then_inc(s_dve, 1)
                    n += 1
            dve.wait_ge(s_dve, n)
            nc.vector.tensor_scalar(a, a, 3.1415925, -3.1415925, ALU.min, ALU.max).then_inc(s_dve, 1)
            dve.wait_ge(s_dve, n + 1)
            nc.vector.scalar_tensor_tensor(t, a, -1.0, a, ALU.mult, ALU.max).then_inc(s_dve, 1)
            dve.wait_ge(s_dve, n + 2)
            nc.vector.tensor_scalar(t, t, -1.0, math.pi / 2, ALU.mult, ALU.add).then_inc(s_reduced, 1)

            with dve.Fori(0, L) as l:
                split_rest(l, 0, 0)
                h_norm(l, "mix_pre")
                project(l, "misc")
                project(l, "nsa")
                nc.vector.memset(kg32[:, :, NC:NCP], 0.0)
                nc.vector.memset(vc_feat[:, NC:NCP], 0.0)
                for cv in range(2):
                    wait_chunk_read(dve, l, "nsa", 9)
                    if cv == 1:
                        dve.wait_ge(part_ready, l * NPT + 1)
                    src = proj[:, PJ_K["cmp"] + cv, :]
                    for n in range(2):
                        nc.vector.tensor_copy(block_in[:, n * CMP_STRIDE:(n + 1) * CMP_STRIDE, 0:NC],
                                              src[:, n * CMP_STRIDE:n * CMP_STRIDE + NC * CMP_STRIDE].rearrange(
                                                  "p (c n) -> p n c", n=CMP_STRIDE)).then_inc(blocks_tok, 1)
                    nc.vector.tensor_copy(block_in[:, :, NC],
                                          cmp_pe[:, bass.ds(l * (2 * CMP_LEN) + cv * CMP_LEN, CMP_LEN)]).then_inc(blocks_tok, 1)
                    c = CB["cmp"] + cv
                    dve.wait_ge(part_ready, l * NPT + (cv + 1))
                    if cv == 0:
                        for kv in range(KVH):
                            g = slice(kv * HD, (kv + 1) * HD)
                            ins = nc.vector.tensor_scalar(kg32[:, kv, 0:NC], acc[c % 2][g, 0:NC], acc[c % 2][g, NC:NCP],
                                                          None, ALU.add)
                        ins.then_inc(acc_free[c % 2], 1)
                    else:
                        nc.vector.tensor_scalar(vc_feat[:, 0:NC], acc[c % 2][:, 0:NC], acc[c % 2][:, NC:NCP], None,
                                                ALU.add).then_inc(acc_free[c % 2], 1)
                dve.wait_ge(ng_tanh, l + 1)
                for h in range(3):
                    ins = nc.vector.tensor_scalar(coef[:, h, :, :], gate_tanh[:, :, h:3 * H:3], 0.5, 0.5, ALU.mult, ALU.add)
                ins.then_inc(ng_coef, 1)
                dve.wait_ge(ng_coef, l * 2 + 1)
                nc.vector.tensor_tensor(coef[:, 0, :, :], coef[:, 0, :, :],
                                        row_sees[:, :].unsqueeze(2).to_broadcast([P, NT, H]), ALU.mult).then_inc(ng_coef, 1)
                value_turns(l, "v_cmp", 1, NCP, 1)
                attend(l, CMP)
                value_turns(l, "v_sel", 1, P, NT)
                attend(l, SEL, PJ_K["sel"])
                value_turns(l, "v_win", 1, P, NT)
                attend(l, WIN, PJ_K["win"])
                dve.sem_inc(gated, 4 * (NHD - HB["swa"]))
                branch(l, 0)
                project(l, "swa")
                wait_chunk_read(dve, l, "swa", 5)
                value_turns(l, "v_swa", 1, P, NT)
                attend(l, SWA, PJ_K["swa"])
                dve.sem_inc(sink_added, 4 * (NHD - HB["mla"]))
                branch(l, 1)
                project(l, "mla")
                wait_chunk_read(dve, l, "mla", 2)
                norm(l, "mlaq", QR, lambda c: proj[:, PJ_CQ + c, :], lambda c: y_hi[:, c, :], lambda c: y_lo[:, c, :])
                norm(l, "mlakv", KVR, lambda c: proj[:, PJ_CQ + 2, :], lambda c: y_hi[:, 2, :], lambda c: y_lo[:, 2, :])
                project(l, "qup")
                project(l, "kvup")
                rotate(l, 0, narrow[r, :])
                wait_chunk_read(dve, l, "qup", 7)
                for h in range(H):
                    rotate(l, 1 + h, proj[r, h, :])
                for e in range(2):
                    dve.wait_ge(rot_high, l * 2 + (e + 1))
                    dve.wait_ge(rope, l * 36 + 37)
                    nc.vector.tensor_tensor(k_lo[HD:HD + ROT, e, :], narrow[r, :], k_hi[HD:HD + ROT, e, :].bitcast(F32),
                                            ALU.subtract)
                value_turns(l, "v_mla", 4, P, NT)
                attend(l, MLA)
                branch(l, 2)
                project(l, "fox")
                at = l * 9
                nc.vector.tensor_scalar(cum, narrow[R_F:R_F + H, :], f_bias[:, bass.ds(l, 1)], None,
                                        ALU.add).then_inc(forget, 1)
                dve.wait_ge(forget, at + 1)
                nc.vector.scalar_tensor_tensor(logit, cum, -1.0, cum, ALU.mult, ALU.max).then_inc(forget, 1)
                dve.wait_ge(forget, at + 2)
                nc.vector.tensor_scalar(cum, cum, 0.0, None, ALU.min).then_inc(forget, 1)
                nc.vector.memset(cum_rows[:, :].bitcast(F32), 0.0).then_inc(forget, 1)
                dve.wait_ge(forget_act, l * 2 + 2)
                dve.wait_ge(forget, at + 4)
                nc.vector.tensor_tensor(logit, cum, softplus, ALU.subtract).then_inc(forget, 1)
                dve.wait_ge(forget, at + 5)
                nc.vector.tensor_tensor_scan(cum, logit, logit, 0.0, ALU.add, ALU.bypass).then_inc(forget, 1)
                dve.wait_ge(forget, at + 6)
                for b in range(0, P, 2 * 32):
                    nc.vector.tensor_copy(cum_rows[b:b + H, :], cum).then_inc(forget, 1)
                dve.wait_ge(forget, at + 8)
                for b in range(32, P, 2 * 32):
                    ins = nc.vector.tensor_tensor(cum_rows[b:b + H, :], cum, cum_rows[0:H, :].bitcast(F32), ALU.subtract)
                ins.then_inc(forget, 1)
                value_turns(l, "v_fox", 4, P, NT)
                attend(l, FOX)
                branch(l, 3)
                for c in range(KT):
                    rest_of_chunk(l, "merged", c, h_lo[:, c, :], trunk[:, c, :], h_hi[:, c, :])
                project(l, "wout")
                dve.wait_ge(x_back, l * 16 + 16)
                add_to_trunk(l, "mix_post", "wout")
                h_norm(l, "xa_pre")
                dve.wait_ge(mem_back, l * 16 + 16)
                for c in range(KT + 1):
                    if c < KT:
                        dve.wait_ge(split_ready, l * NSP + (SPB["mem"] + c - 1))
                        nc.vector.tensor_scalar(work[:, c % 2, 0:M], m_f32[:, c, :], gain(l, "mem", c), None,
                                                ALU.mult).then_inc(split_in, 1)
                    if c > 0:
                        rest_of_chunk(l, "mem", c - 1, m_lo[:, c - 1, :], work[:, (c - 1) % 2, 0:M], m_hi[:, c - 1, :])
                project(l, "xq")
                project(l, "xkv")
                wait_chunk_read(dve, l, "xkv", 3)
                value_turns(l, "v_xa", 2, P, MT)
                attend(l, XA)
                project(l, "xo")
                add_to_trunk(l, "xa_post", "xo")
                h_norm(l, "ffn_pre")

                def ff(j):
                    c = CB["ffin"]
                    next_unit(l, "ffin", 0, j)
                    dve.wait_ge(ff_tanh, l * FK + j + 1)
                    nc.vector.scalar_tensor_tensor(work[:, 0, :], work[:, 0, :], 1.0, acc[c % 2][:, :], ALU.add,
                                                   ALU.mult).then_inc(acc_free[c % 2], 1)
                    next_unit(l, "ffin", 1, j)
                    wait_chunk(dve, l, "ffin", 1, j, 0)
                    dve.wait_ge(acc_free[c % 2], free_at(l, c, 1, j) + 1)
                    nc.vector.scalar_tensor_tensor(work[:, 0, :], work[:, 0, :], 0.5, acc[(c + 1) % 2][:, :], ALU.mult,
                                                   ALU.mult).then_inc(acc_free[(c + 1) % 2], 1)
                    dve.wait_ge(split_high, l * NSP + j + (SPB["ffa"] + 1))
                    a = a_hi[:, bass.ds(j, 1), :]
                    nc.vector.tensor_tensor(a_lo[:, bass.ds(j, 1), :], work[:, 0, :], a.bitcast(F32),
                                            ALU.subtract).then_inc(split_ready, 1)
                with dve.Fori(0, FK) as j:
                    ff(j)
                for n in range(3 * KT - 1):
                    next_unit(l, "ffout", n, 0)
                add_to_trunk(l, "ffn_post", "ffout")


_INS = ["x", "mem", "positions", "mix_norm_pre", "w_in", "nsa_cmp_w", "nsa_cmp_pe", "swa_sinks", "mla_q_norm",
        "mla_w_q_up", "mla_kv_norm", "mla_w_kv_up", "fox_f_bias", "w_branch", "w_gate", "w_out", "mix_norm_post",
        "xa_norm_pre", "xa_mem_norm", "xa_w_q", "xa_w_kv", "xa_w_o", "xa_norm_post", "ffn_norm_pre", "ffn_w_in",
        "ffn_w_out", "ffn_norm_post"]


def kernel(**inputs):
    import concourse.bacc as bacc
    from concourse.bass_utils import run_bass_kernel_spmd

    nc = bacc.Bacc("TRN2", target_bir_lowering=False, num_devices=1)
    arrays, args = {}, []
    for name in _INS:
        a = np.ascontiguousarray(inputs[name])
        arrays[f"in_{name}_dram"] = a
        args.append(nc.dram_tensor(f"in_{name}_dram", a.shape, mybir.dt.from_np(a.dtype), kind="ExternalInput").ap())
    args.append(nc.dram_tensor("out_dram", (1, S, D), F32, kind="ExternalOutput").ap())
    build(nc, *args)
    r = run_bass_kernel_spmd(nc, [arrays], core_ids=[0])
    return r.results[0]["out_dram"]
```
